# Optimizing a Trainium2 kernel written in Bass

```python
import math
import jax, jax.numpy as jnp
from jax import lax
import numpy as np

D_MODEL = 2048
BATCH = 1
SEQ = 256
DEPTH = 2

N_MIXERS = 2
PLE_DIM = 256
NORM_EPS = 1e-6

SSM_EXPAND = 2
D_INNER = SSM_EXPAND * D_MODEL
SSM_HEAD_DIM = 64
SSM_HEADS = D_INNER // SSM_HEAD_DIM
SSM_GROUPS = 8
SSM_STATE = 128
CONV_WIDTH = 4
SSD_CHUNK = 128
CONV_CH = D_INNER + 2 * SSM_GROUPS * SSM_STATE
SSM_IN_DIM = 2 * D_INNER + 2 * SSM_GROUPS * SSM_STATE + SSM_HEADS

ATTN_HEADS = 16
ATTN_HEAD_DIM = D_MODEL // ATTN_HEADS
MOBA_BLOCK = 256
MOBA_TOPK = 3
MOBA_Q_CHUNK = 16

FFN_HIDDEN = ((8 * D_MODEL + 3 * 256 - 1) // (3 * 256)) * 256

N_SSM_LAYERS = (DEPTH + 1) // 2
N_ATTN_LAYERS = DEPTH // 2

kernel_name = "hybrid_mamba2_moba_block"

def rmsnorm(x, g):
    xf = x.astype(jnp.float32)
    y = xf * lax.rsqrt(jnp.mean(xf * xf, axis=-1, keepdims=True) + NORM_EPS)
    return (y * g.astype(jnp.float32)).astype(x.dtype)

def causal_dwconv(u, w, b):
    c = u.shape[-1]
    y = lax.conv_general_dilated(u, w[:, None, :].astype(u.dtype), window_strides=(1,),
                                 padding=[(CONV_WIDTH - 1, 0)],
                                 dimension_numbers=('NWC', 'WIO', 'NWC'),
                                 feature_group_count=c)
    return y + b.astype(u.dtype)

def segsum(a):
    t = a.shape[-1]
    cs = jnp.cumsum(a, axis=-1)
    diff = cs[..., :, None] - cs[..., None, :]
    mask = jnp.tril(jnp.ones((t, t), dtype=bool))
    return jnp.where(mask, diff, -jnp.inf)

def ssd_chunked(xdt, a, bm, cm):
    b, l, h, p = xdt.shape
    g, n = bm.shape[2], bm.shape[3]
    r = h // g
    nc = l // SSD_CHUNK
    xc = xdt.reshape(b, nc, SSD_CHUNK, g, r, p)
    ac = a.astype(jnp.float32).reshape(b, nc, SSD_CHUNK, g, r).transpose(0, 3, 4, 1, 2)
    bc = bm.reshape(b, nc, SSD_CHUNK, g, n)
    cc = cm.reshape(b, nc, SSD_CHUNK, g, n)
    a_cs = jnp.cumsum(ac, axis=-1)
    decay = jnp.exp(segsum(ac))
    cb = jnp.einsum('bclgn,bcsgn->bcgls', cc, bc)
    y_diag = jnp.einsum('bcgls,bgrcls,bcsgrp->bclgrp', cb, decay, xc)
    decay_states = jnp.exp(a_cs[..., -1:] - a_cs)
    chunk_states = jnp.einsum('bclgn,bgrcl,bclgrp->bcgrpn', bc, decay_states, xc).astype(jnp.float32)
    chunk_decay = jnp.exp(a_cs[..., -1])

    def step(state, inp):
        s_c, d_c = inp
        new = state * d_c[..., None, None] + s_c
        return new, state

    h0 = jnp.zeros((b, g, r, p, n), jnp.float32)
    _, states_in = lax.scan(step, h0, (jnp.moveaxis(chunk_states, 1, 0), jnp.moveaxis(chunk_decay, 3, 0)))
    y_off = jnp.einsum('bclgn,cbgrpn,bgrcl->bclgrp', cc, states_in, jnp.exp(a_cs))
    return (y_diag + y_off).reshape(b, l, h, p)

def mamba2_mixer(u, w_in, conv_w, conv_b, dt_bias, a_log, d_skip, norm_g, w_out):
    b, l, _ = u.shape
    zxbcdt = u @ w_in
    z, xbc, dt = jnp.split(zxbcdt, [D_INNER, D_INNER + CONV_CH], axis=-1)
    xbc = jax.nn.silu(causal_dwconv(xbc, conv_w, conv_b))
    xs, bm, cm = jnp.split(xbc, [D_INNER, D_INNER + SSM_GROUPS * SSM_STATE], axis=-1)
    xs = xs.reshape(b, l, SSM_HEADS, SSM_HEAD_DIM)
    bm = bm.reshape(b, l, SSM_GROUPS, SSM_STATE)
    cm = cm.reshape(b, l, SSM_GROUPS, SSM_STATE)
    dt = jax.nn.softplus(dt.astype(jnp.float32) + dt_bias.astype(jnp.float32))
    a = -jnp.exp(a_log.astype(jnp.float32))
    y = ssd_chunked(xs * dt[..., None].astype(xs.dtype), dt * a, bm, cm)
    y = (y + d_skip[:, None] * xs).reshape(b, l, D_INNER)
    yg = (y * jax.nn.silu(z)).astype(jnp.float32).reshape(b, l, SSM_GROUPS, D_INNER // SSM_GROUPS)
    yg = yg * lax.rsqrt(jnp.mean(yg * yg, axis=-1, keepdims=True) + NORM_EPS)
    y = (yg.reshape(b, l, D_INNER) * norm_g.astype(jnp.float32)).astype(u.dtype)
    return y @ w_out

def moba_attention(u, w_qkv, w_o):
    b, l, _ = u.shape
    hh, dh, bs, qc = ATTN_HEADS, ATTN_HEAD_DIM, MOBA_BLOCK, MOBA_Q_CHUNK
    qkv = (u @ w_qkv).reshape(b, l, 3, hh, dh)
    q = qkv[:, :, 0].transpose(0, 2, 1, 3)
    k = qkv[:, :, 1].transpose(0, 2, 1, 3)
    v = qkv[:, :, 2].transpose(0, 2, 1, 3)
    nb = -(-l // bs)
    lp = nb * bs
    pad = ((0, 0), (0, 0), (0, lp - l), (0, 0))
    q, k, v = jnp.pad(q, pad), jnp.pad(k, pad), jnp.pad(v, pad)
    k_blk = k.reshape(b, hh, nb, bs, dh)
    v_blk = v.reshape(b, hh, nb, bs, dh)
    k_mean = jnp.mean(k_blk.astype(jnp.float32), axis=3)
    gate = jnp.einsum('bhtd,bhnd->bhtn', q.astype(jnp.float32), k_mean)
    q_block = jnp.arange(lp) // bs
    past = jnp.arange(nb)[None, :] < q_block[:, None]
    gate = jnp.where(past, gate, -jnp.inf)
    kk = min(MOBA_TOPK, nb)
    sel_val, sel_idx = lax.top_k(gate, kk)
    sel_ok = sel_val > -jnp.inf

    nq = lp // qc

    def to_chunks(t):
        t = t.reshape(b, hh, nq, qc, *t.shape[3:])
        return jnp.moveaxis(t, 2, 0)

    scale = dh ** -0.5
    bi = jnp.arange(b)[:, None, None, None]
    hi = jnp.arange(hh)[None, :, None, None]

    def attend(args):
        c, q_c, idx_c, ok_c = args
        t_pos = c * qc + jnp.arange(qc)
        own = (c * qc) // bs
        k_own = lax.dynamic_index_in_dim(k_blk, own, axis=2, keepdims=False)
        v_own = lax.dynamic_index_in_dim(v_blk, own, axis=2, keepdims=False)
        s_pos = own * bs + jnp.arange(bs)
        s_own = jnp.einsum('bhqd,bhsd->bhqs', q_c, k_own).astype(jnp.float32) * scale
        s_own = jnp.where(s_pos[None, :] <= t_pos[:, None], s_own, -jnp.inf)
        k_sel = k_blk[bi, hi, idx_c]
        v_sel = v_blk[bi, hi, idx_c]
        s_sel = jnp.einsum('bhqd,bhqksd->bhqks', q_c, k_sel).astype(jnp.float32) * scale
        s_sel = jnp.where(ok_c[..., None], s_sel, -jnp.inf)
        logits = jnp.concatenate([s_own, s_sel.reshape(b, hh, qc, kk * bs)], axis=-1)
        pr = jax.nn.softmax(logits, axis=-1).astype(v_blk.dtype)
        p_own = pr[..., :bs]
        p_sel = pr[..., bs:].reshape(b, hh, qc, kk, bs)
        return (jnp.einsum('bhqs,bhsd->bhqd', p_own, v_own)
                + jnp.einsum('bhqks,bhqksd->bhqd', p_sel, v_sel))

    o = lax.map(attend, (jnp.arange(nq), to_chunks(q), to_chunks(sel_idx), to_chunks(sel_ok)))
    o = jnp.moveaxis(o, 0, 2).reshape(b, hh, lp, dh)[:, :, :l]
    o = o.transpose(0, 2, 1, 3).reshape(b, l, hh * dh)
    return o @ w_o

def swiglu(u, w_gate, w_up, w_down):
    return (jax.nn.silu(u @ w_gate) * (u @ w_up)) @ w_down

def setup_inputs(seed: int = 0) -> dict:
    key = jax.random.key(seed)
    ks = jax.random.split(key, 24)
    f32 = jnp.float32

    def nrm(k, shape, fan_in):
        return jax.random.normal(k, shape, f32) * (fan_in ** -0.5)

    def gain(k, shape):
        return 1.0 + 0.05 * jax.random.normal(k, shape, f32)

    ns, na = N_SSM_LAYERS, N_ATTN_LAYERS
    dt0 = jnp.exp(jax.random.uniform(ks[8], (ns, SSM_HEADS), f32, math.log(1e-3), math.log(1e-1)))
    dt_bias = dt0 + jnp.log(-jnp.expm1(-dt0))
    a_log = jnp.log(jax.random.uniform(ks[9], (ns, SSM_HEADS), f32, 1.0, 16.0))
    return {
        "x": jax.random.normal(ks[0], (BATCH, SEQ, D_MODEL), f32),
        "p": jax.random.normal(ks[1], (DEPTH, BATCH, SEQ, PLE_DIM), f32),
        "mix_norm_g": gain(ks[2], (DEPTH, D_MODEL)),
        "ffn_norm_g": gain(ks[3], (DEPTH, D_MODEL)),
        "ple_norm_g": gain(ks[4], (DEPTH, D_MODEL)),
        "ssm_w_in": nrm(ks[5], (ns, D_MODEL, SSM_IN_DIM), D_MODEL),
        "ssm_conv_w": nrm(ks[6], (ns, CONV_WIDTH, CONV_CH), CONV_WIDTH),
        "ssm_conv_b": 0.01 * jax.random.normal(ks[7], (ns, CONV_CH), f32),
        "ssm_dt_bias": dt_bias,
        "ssm_a_log": a_log,
        "ssm_d": 1.0 + 0.1 * jax.random.normal(ks[10], (ns, SSM_HEADS), f32),
        "ssm_norm_g": gain(ks[11], (ns, D_INNER)),
        "ssm_w_out": nrm(ks[12], (ns, D_INNER, D_MODEL), D_INNER),
        "attn_w_qkv": nrm(ks[13], (na, D_MODEL, 3 * ATTN_HEADS * ATTN_HEAD_DIM), D_MODEL),
        "attn_w_o": nrm(ks[14], (na, ATTN_HEADS * ATTN_HEAD_DIM, D_MODEL), D_MODEL),
        "ffn_w_gate": nrm(ks[15], (DEPTH, D_MODEL, FFN_HIDDEN), D_MODEL),
        "ffn_w_up": nrm(ks[16], (DEPTH, D_MODEL, FFN_HIDDEN), D_MODEL),
        "ffn_w_down": nrm(ks[17], (DEPTH, FFN_HIDDEN, D_MODEL), FFN_HIDDEN),
        "ple_w_proj": nrm(ks[18], (DEPTH, PLE_DIM, D_MODEL), PLE_DIM),
        "ple_w_gate": nrm(ks[19], (DEPTH, D_MODEL, D_MODEL), D_MODEL),
        "final_norm_g": gain(ks[20], (D_MODEL,)),
    }

def reference(x, p, mix_norm_g, ffn_norm_g, ple_norm_g, ssm_w_in, ssm_conv_w, ssm_conv_b,
              ssm_dt_bias, ssm_a_log, ssm_d, ssm_norm_g, ssm_w_out, attn_w_qkv, attn_w_o,
              ffn_w_gate, ffn_w_up, ffn_w_down, ple_w_proj, ple_w_gate, final_norm_g):
    h = x
    for i in range(DEPTH):
        u = rmsnorm(h, mix_norm_g[i])
        j = i // N_MIXERS
        if i % N_MIXERS == 0:
            mix = mamba2_mixer(u, ssm_w_in[j], ssm_conv_w[j], ssm_conv_b[j], ssm_dt_bias[j],
                               ssm_a_log[j], ssm_d[j], ssm_norm_g[j], ssm_w_out[j])
        else:
            mix = moba_attention(u, attn_w_qkv[j], attn_w_o[j])
        h = h + mix
        h = h + swiglu(rmsnorm(h, ffn_norm_g[i]), ffn_w_gate[i], ffn_w_up[i], ffn_w_down[i])
        gate = jax.nn.sigmoid(rmsnorm(h, ple_norm_g[i]) @ ple_w_gate[i])
        h = h + gate * (p[i] @ ple_w_proj[i])
    return rmsnorm(h, final_norm_g)


_drawn_inputs = setup_inputs


def setup_inputs(seed=0):
    import zlib

    import numpy as np

    out = dict(_drawn_inputs(seed))
    spreads = {}
    factors = {'ple_norm_g': 6.449, 'ssm_conv_b': 5.327}
    for name, (base, spread) in spreads.items():
        noise = np.random.default_rng([zlib.crc32(name.encode()), seed]).standard_normal(out[name].shape)
        drawn = base * np.exp(spread * noise) if base else spread * noise
        out[name] = __import__('jax').numpy.asarray(drawn.astype(out[name].dtype))
    for name, factor in factors.items():
        out[name] = (out[name] * factor).astype(out[name].dtype)
    return out
```

```python
from contextlib import ExitStack

import concourse.bass as bass
from concourse import mybir

F32 = mybir.dt.float32
F32R = mybir.dt.float32r
BF16 = mybir.dt.bfloat16
ALU = mybir.AluOpType
ACT = mybir.ActivationFunctionType
AX = mybir.AxisListType

P = 128
TOK = 2
RING = 4
CK = 2
BLK = 512
BT = BLK // P
CONV = 4
EPS = 1e-6
NEG = -1.0e30
AHEAD = 5


class Steps:

    def __init__(self):
        self.base, self.k, self.i, self.per = 0, 0, 0, 0

    def next(self):
        self.k += 1
        return self.last()

    def last(self, back=0):
        return self.base + self.k - back + (self.i * self.per if self.per else 0)

    def enter(self, i, per):
        self.base, self.k, self.i, self.per = self.base + self.k, 0, i, per

    def leave(self, times):
        assert self.k == self.per or not self.per, (self.k, self.per)
        self.base, self.k, self.i, self.per = self.base + self.k * times, 0, 0, 0


def trunk(nc, x, p, mix_norm_g, ffn_norm_g, ple_norm_g, ssm_w_in, ssm_conv_w, ssm_conv_b, ssm_dt_bias,
          ssm_a_log, ssm_d, ssm_norm_g, ssm_w_out, attn_w_qkv, attn_w_o, ffn_w_gate, ffn_w_up, ffn_w_down,
          ple_w_proj, ple_w_gate, final_norm_g, out, cs_scratch):
    D = x.shape[2]
    KD = D // P
    NB = D // BLK
    DI = ssm_w_out.shape[1]
    KI = DI // P
    SH = ssm_d.shape[1]
    HD = DI // SH
    G = 8
    HG = SH // G
    CH = ssm_conv_w.shape[2]
    CT = CH // P
    F = ffn_w_gate.shape[2]
    KF = F // P
    FB = F // BLK
    AH = attn_w_o.shape[1] // P
    PD = p.shape[3]
    KP = PD // P
    SCALE = float(P) ** -0.5
    assert TOK * P == x.shape[1] and KP == CK and HG * HD == BLK and BT == 4

    full = [CK] * (KD // CK)
    inner = [CK] * (KI // CK)
    hidden = [CK] * 20 + [1] * 4
    assert sum(hidden) == KF and len(hidden) % RING == 0

    order = [("xbc", CH // BLK, len(full)), ("z", G, len(full)), ("wout", NB, len(inner)),
             ("gu0", 2 * FB, len(full)), ("down0", NB, len(hidden)), ("pp0", 2, 2), ("ple0", NB, len(full)),
             ("v", NB, len(full)), ("qk", 2 * NB, len(full)), ("wo", NB, len(full)),
             ("gu1", 2 * FB, len(full)), ("down1", NB, len(hidden)), ("pp1", 2, 2), ("ple1", NB, len(full))]
    CHUNK, JOB, M, c, j = {}, {}, {}, 0, 0
    for name, jobs, m in order:
        CHUNK[name], JOB[name], M[name] = c, j, m
        c, j = c + jobs * m, j + jobs
        assert c % RING == 0
    CHUNKS = c
    TURN = {"first": 0, "xbc": 4, "z": 16, "wout": 24, "gu0": 28, "down0": 28 + FB}
    TURN["ple0"] = TURN["down0"] + NB
    TURN["q0"] = TURN["ple0"] + NB
    TURN["qk"] = TURN["q0"] + 1
    TURN["k3"] = TURN["qk"] + 3 * (NB - 1)
    TURN["o3"] = TURN["k3"] + 1
    TURN["wo"] = TURN["o3"] + 1
    TURN["gu1"] = TURN["wo"] + NB
    TURN["down1"] = TURN["gu1"] + FB
    FILL = {"xbc": 0, "z": 12, "wout": 20, "gu0": 24, "down0": 24 + FB}
    FILL["ple0"] = FILL["down0"] + NB
    FILL["qk"] = FILL["ple0"] + NB
    FILL["wo"] = FILL["qk"] + 2 * NB
    FILL["gu1"] = FILL["wo"] + NB
    FILL["down1"] = FILL["gu1"] + FB
    FILL["ple1"] = FILL["down1"] + NB
    UPDATE = {"wout": 0, "down0": 1, "ple0": 2, "wo": 3, "down1": 4, "ple1": 5}

    with ExitStack() as ctx:
        KB = 1024
        base = (nc.sbuf_base + 63) // 64 * 64
        ARENA = (nc.sbuf_bytes_remaining - 256) // 64 * 64
        ctx.enter_context(nc.sbuf_tensor("arena", [P, ARENA // 4 + 16], F32))
        at = [0]

        def place(name, shape, off=None, dt=F32):
            size = mybir.dt.size(dt)
            for n in shape[1:]:
                size *= n
            if off is None:
                off = at[0]
                at[0] += (size + 31) // 32 * 32
            assert off + size <= ARENA, (name, off + size)
            return nc.alloc_sbuf_tensor_at(name, shape, dt, offset=base + off)

        def sem(name):
            return ctx.enter_context(nc.semaphore(name))

        h = place("h", [P, TOK, D])
        raw = place("raw", [P, RING, CK, BLK])
        wh = place("wh", [P, RING, CK, BLK], dt=F32R)
        wl = place("wl", [P, RING, CK, BLK], dt=F32R)
        uh = place("uh", [P, KD, TOK * P], dt=F32R)
        ul = place("ul", [P, KD, TOK * P], dt=F32R)
        stage = place("stage", [P, TOK, BLK])
        ident = place("ident", [P, P])
        mask = place("mask", [P, P])
        gains = place("gains", [P, P])
        ssq = place("ssq", [P, TOK, NB])
        pair = place("pair", [P, TOK, 2])
        mean = place("mean", [P, TOK])
        rstd = place("rstd", [P, TOK])
        neghalf = place("neghalf", [P, TOK])
        junk = place("junk", [P, BLK], dt=BF16)
        conv = place("conv", [P, CONV + 1, CT])
        dt_ = place("dt", [P, TOK, SH])
        cs = place("cs", [P, TOK, SH])
        ecs = place("ecs", [P, SH])
        skip = place("skip", [P, SH])
        gsq = place("gsq", [P, TOK])
        gmean = place("gmean", [P, TOK])
        grstd = place("grstd", [P, TOK])
        big = at[0]
        work = big + 80 * KB
        at[0] = work
        dec = place("dec", [P, TOK, HG, P])
        xdt = place("xdt", [P, TOK, HG, HD])
        xw = place("xw", [P, HG, HD])
        bg = place("bg", [P, TOK * P])
        cg = place("cg", [P, TOK * P])
        btok = place("btok", [P, P])
        xs = place("xs", [P, TOK, HG, HD])
        chan = place("chan", [P, BT, TOK * P], off=work + 8 * KB)
        state = place("state", [P, BLK], off=work + 12 * KB)
        top_of_work = at[0]
        side_at = big + 88 * KB
        xc = place("xc", [P, DI // P, TOK * P], off=big + 32 * KB)
        bc = place("bc", [P, 2 * G, TOK * P], off=big + 64 * KB)
        yt = place("yt", [P, G, 2, BT, TOK * P], off=big, dt=F32R)
        hh = place("hh", [P, KF, TOK * P], off=big, dt=F32R)
        hl = place("hl", [P, KF, TOK * P], off=big + 44 * KB, dt=F32R)
        pp = place("pp", [P, TOK, D], off=big)
        pt = place("pt", [P, KP, TOK * P], off=big + 16 * KB)
        ph = place("ph", [P, KP, TOK * P], off=side_at, dt=F32R)
        pl = place("pl", [P, KP, TOK * P], off=side_at + 2 * KB, dt=F32R)
        prow = place("prow", [P, TOK, PD], off=side_at + 4 * KB)
        vh = place("vh", [P, KD, TOK * P], off=big + 16 * KB, dt=F32R)
        vl = place("vl", [P, KD, TOK * P], off=big + 32 * KB, dt=F32R)
        v = place("v", [P, TOK, D], off=big)
        oh = place("oh", [P, KD, TOK * P], off=big + 48 * KB, dt=F32R)
        ol = place("ol", [P, KD, TOK * P], off=big + 64 * KB, dt=F32R)
        qt = place("qt", [P, BT, TOK * P], off=big + 80 * KB)
        kt = place("kt", [P, BT, TOK * P], off=big + 84 * KB)
        sc = place("sc", [P, 2, 3 * P], off=side_at)
        prt = place("prt", [P, 2, 3, P], off=side_at + 3 * KB)
        orow = place("orow", [P, TOK, BLK], off=side_at + 6 * KB)
        mask3 = place("mask3", [P, 3 * P], off=side_at + 10 * KB)
        top = place("top", [P, BT, 2], off=side_at + 12 * KB)
        ntop = place("ntop", [P, BT, 2], off=side_at + 12 * KB + 64)
        den = place("den", [P, BT, 2], off=side_at + 12 * KB + 128)
        rden = place("rden", [P, BT, 2], off=side_at + 12 * KB + 192)
        fgain = place("fgain", [P, D], off=big + 64 * KB)
        grows = place("grows", [P, P], off=big)
        crows = place("crows", [CT, CONV + 1, P], off=big + 1 * KB)
        draw = place("draw", [P, KD, SH], off=big + 4 * KB)
        dwh = place("dwh", [P, KD, SH], off=big + 8 * KB, dt=F32R)
        dwl = place("dwl", [P, KD, SH], off=big + 12 * KB, dt=F32R)
        upper = place("upper", [P, P], off=big + 16 * KB)
        dtb = place("dtb", [P, SH], off=big + 17 * KB)
        alog = place("alog", [P, SH], off=big + 17 * KB + 256)
        nega = place("nega", [P, SH], off=big + 17 * KB + 512)
        dx = place("dx", [P, TOK * SH], off=big + 18 * KB)
        dabs = place("dabs", [P, TOK * SH], off=big + 18 * KB + 512)
        dexp = place("dexp", [P, TOK * SH], off=big + 19 * KB)
        drel = place("drel", [P, TOK * SH], off=big + 19 * KB + 512)
        dden = place("dden", [P, TOK * SH], off=big + 20 * KB)
        drec = place("drec", [P, TOK * SH], off=big + 20 * KB + 512)
        dy = place("dy", [P, TOK * SH], off=big + 21 * KB)
        dy2 = place("dy2", [P, TOK * SH], off=big + 21 * KB + 512)
        dq = [place(f"dq{n}", [P, TOK * SH], off=big + 22 * KB + 512 * n) for n in range(2)]
        dta = place("dta", [P, TOK, SH], off=big + 23 * KB)
        cst = place("cst", [P, P], off=big + 23 * KB + 512)
        assert top_of_work <= ARENA and side_at + 13 * KB <= ARENA

        def bank(name, shape):
            return ctx.enter_context(nc.psum_tensor(name, shape, F32))

        acc = [bank("acc0", [P, BLK]), bank("acc1", [P, BLK])]
        turned = bank("turned", [P, BT, TOK * P])
        pg = bank("pg", [P, BLK])
        pst = bank("pst", [P, BLK])
        py = bank("py", [P, TOK, BLK])

        load = [sem(f"load{s}") for s in range(RING)]
        hi_done = sem("hi_done")
        lo_done = sem("lo_done")
        mm_done = sem("mm_done")
        acc_done = sem("acc_done")
        acc_free = [sem("acc_free0"), sem("acc_free1")]
        filled = sem("filled")
        turn = sem("turn")
        turn_act = sem("turn_act")
        turn_dve = sem("turn_dve")
        gate_in = sem("gate_in")
        squares = sem("squares")
        h_kept = sem("h_kept")
        rstd_ready = sem("rstd_ready")
        act_step, dve_step, pool_step = sem("act_step"), sem("dve_step"), sem("pool_step")
        consts = sem("consts")
        x_in = [sem(f"x_in{b}") for b in range(NB)]
        small_in = sem("small_in")
        dt_in = sem("dt_in")
        bias_in = sem("bias_in")
        gain_turn, gain_kept = sem("gain_turn"), sem("gain_kept")
        dt_hi, dt_lo, dt_mm = sem("dt_hi"), sem("dt_lo"), sem("dt_mm")
        dt_x, dt_act, dta_done = sem("dt_x"), sem("dt_act"), sem("dta_done")
        cs_mm, cs_kept, cs_out, ecs_done = sem("cs_mm"), sem("cs_kept"), sem("cs_out"), sem("ecs_done")
        conv_bias, conv_taps, conv_out = sem("conv_bias"), sem("conv_taps"), sem("conv_out")
        taps_seen = sem("taps_seen")
        group_in, dec_in, dec_masked = sem("group_in"), sem("dec_in"), sem("dec_masked")
        x_turn, bg_turn, x_kept, b_kept = sem("x_turn"), sem("bg_turn"), sem("x_kept"), sem("b_kept")
        xdt_done, skip_done, diff_done, exp_done = sem("xdt_done"), sem("skip_done"), sem("diff_done"), sem("exp_done")
        xw_done, m_done, pg_free = sem("xw_done"), sem("m_done"), sem("pg_free")
        st_mm, st_kept, yoff_mm = sem("st_mm"), sem("st_kept"), sem("yoff_mm")
        ssd_done = sem("ssd_done")
        y_taken = sem("y_taken")
        gated, g_squares, g_rstd, g_squares_step = sem("gated"), sem("g_squares"), sem("g_rstd"), sem("g_squares_step")
        p_in, p_turn, p_hi, p_lo = sem("p_in"), sem("p_turn"), sem("p_hi"), sem("p_lo")
        side_kept = sem("side_kept")
        s_mm, s_top, s_exp = sem("s_mm"), sem("s_top"), sem("s_exp")
        pr_turn, pr_kept, o_mm, o_kept = sem("pr_turn"), sem("pr_kept"), sem("o_mm"), sem("o_kept")
        fgain_in, out_ready, out_done = sem("fgain_in"), sem("out_ready"), sem("out_done")
        mask3_done = sem("mask3_done")

        def tiles(w):
            return w.rearrange("(k q) n -> q k n", q=P)

        w_in, w_out = tiles(ssm_w_in[0]), tiles(ssm_w_out[0])
        w_gate = [tiles(ffn_w_gate[l]) for l in range(2)]
        w_up = [tiles(ffn_w_up[l]) for l in range(2)]
        w_down = [tiles(ffn_w_down[l]) for l in range(2)]
        w_qkv, w_o = tiles(attn_w_qkv[0]), tiles(attn_w_o[0])
        w_pg = [tiles(ple_w_gate[l]) for l in range(2)]
        w_pp = [tiles(ple_w_proj[l]) for l in range(2)]
        x_rows = x[0].rearrange("(t q) n -> q t n", q=P)
        out_rows = out[0].rearrange("(t q) n -> q t n", q=P)

        def apart(eng):
            eng.wait_ge(consts, 1)

        def bank_ready(eng, t, phase, i):
            if t == 0:
                eng.wait_ge(acc_done, JOB[phase] + i + 1)
            else:
                eng.wait_ge(mm_done, CHUNK[phase] + (i + 1) * M[phase])

        def block_of(tensor, b):
            return tensor[:, :, bass.ds(b * BLK, BLK)]

        GAIN = {"mix0": 0, "mix1": KD, "ffn0": 2 * KD, "ffn1": 3 * KD, "ple0": 4 * KD, "ple1": 5 * KD, "ssm": 6 * KD}

        block = ctx.enter_context(nc.Block())

        @block.sync
        def _(sp):
            def chunk(c, n, src):
                s = n["slot"]
                if n["wait"]:
                    sp.wait_ge(lo_done, c - RING + 1)
                sp.dma_start(raw[:, s, 0:n["tiles"], :], src).then_inc(load[s], 16)

            def job(w, col, c, sizes, first=False):
                k = 0
                for n, size in enumerate(sizes):
                    chunk(c + n, {"slot": n % RING, "wait": not (first and n < RING), "tiles": size},
                          w[:, k:k + size, bass.ds(col, BLK)])
                    k += size

            for b in range(NB):
                sp.dma_start(block_of(h, b), block_of(x_rows, b)).then_inc(x_in[b], 16)
                if b == 0:
                    rows = 0
                    for g in (mix_norm_g, ffn_norm_g, ple_norm_g, ssm_norm_g):
                        n = 2 * KD
                        sp.dma_start(grows[rows:rows + n, :], g.rearrange("l (k q) -> (l k) q", q=P)
                                     ).then_inc(small_in, 16)
                        rows += n
                    sp.dma_start(crows[:, 0:CONV, :], ssm_conv_w[0].rearrange("j (k q) -> k j q", q=P)
                                 ).then_inc(small_in, 16)
                    sp.dma_start(crows[:, CONV, :], ssm_conv_b[0].rearrange("(k q) -> k q", q=P)
                                 ).then_inc(small_in, 16)
            sp.dma_start(draw[:, :, :], w_in[:, :, 2 * DI + 2 * G * P:2 * DI + 2 * G * P + SH]).then_inc(dt_in, 16)
            for dst, src in ((dtb, ssm_dt_bias), (alog, ssm_a_log), (skip, ssm_d)):
                sp.dma_start(dst[:, :], src[0:1, :].broadcast_to([P, SH])).then_inc(bias_in, 16)
            c = CHUNK["xbc"]
            m = len(full)
            job(w_in, 2 * DI, c, full, first=True)
            with sp.Fori(1, 4) as i:
                job(w_in, 2 * DI + i * BLK, c + i * m, full)
            c += 4 * m
            with sp.Fori(0, G) as i:
                job(w_in, DI + i * BLK, c + i * m, full)
            with sp.Fori(0, G) as i:
                job(w_in, i * BLK, CHUNK["z"] + i * m, full)
            with sp.Fori(0, NB) as i:
                job(w_out, i * BLK, CHUNK["wout"] + i * len(inner), inner)
            for l in range(2):
                if l == 1:
                    with sp.Fori(0, NB) as i:
                        job(w_qkv, 2 * D + i * BLK, CHUNK["v"] + i * m, full)
                    with sp.Fori(0, NB) as i:
                        job(w_qkv, i * BLK, CHUNK["qk"] + i * 2 * m, full)
                        job(w_qkv, D + i * BLK, CHUNK["qk"] + i * 2 * m + m, full)
                    with sp.Fori(0, NB) as i:
                        job(w_o, i * BLK, CHUNK["wo"] + i * m, full)
                with sp.Fori(0, FB) as i:
                    job(w_gate[l], i * BLK, CHUNK[f"gu{l}"] + i * 2 * m, full)
                    job(w_up[l], i * BLK, CHUNK[f"gu{l}"] + i * 2 * m + m, full)
                with sp.Fori(0, NB) as i:
                    job(w_down[l], i * BLK, CHUNK[f"down{l}"] + i * len(hidden), hidden)
                for b in range(NB):
                    chunk(CHUNK[f"pp{l}"] + b, {"slot": b % RING, "wait": True, "tiles": CK},
                          w_pp[l][:, :, b * BLK:(b + 1) * BLK])
                with sp.Fori(0, NB) as i:
                    job(w_pg[l], i * BLK, CHUNK[f"ple{l}"] + i * m, full)
            for b in range(NB):
                sp.wait_ge(out_ready, b + 1)
                sp.dma_start(block_of(out_rows, b), block_of(h, b)).then_inc(out_done, 16)
            sp.wait_ge(out_done, NB * 16)

        @block.gpsimd
        def _(pool):
            st = Steps()

            def done():
                pool.wait_ge(pool_step, st.last())

            def step(ins):
                ins.then_inc(pool_step, 1)
                st.next()

            step(pool.memset(ident[:, :], 0.0))
            step(pool.memset(mask[:, :], 0.0))
            step(pool.memset(upper[:, :], 1.0))
            step(pool.memset(neghalf[:, :], -0.5))
            done()
            step(pool.affine_select(out=ident[:, :], in_=ident[:, :], compare_op=ALU.not_equal, fill=1.0,
                                    base=0, pattern=[[-1, P]], channel_multiplier=1))
            step(pool.affine_select(out=mask[:, :], in_=mask[:, :], compare_op=ALU.is_ge, fill=NEG,
                                    base=0, pattern=[[1, P]], channel_multiplier=-1))
            step(pool.affine_select(out=upper[:, :], in_=upper[:, :], compare_op=ALU.is_ge, fill=0.0,
                                    base=0, pattern=[[1, P]], channel_multiplier=-1))
            done()
            pool.nop().then_inc(consts, 1)

            def row_scales(n, sums):
                pool.wait_ge(squares, sums)
                step(pool.tensor_tensor(pair[:, :, :], ssq[:, :, 0:2], ssq[:, :, 2:4], ALU.add))
                done()
                step(pool.tensor_tensor(mean[:, :], pair[:, :, 0], pair[:, :, 1], ALU.add))
                done()
                step(pool.tensor_scalar(mean[:, :], mean[:, :], 1.0 / D, EPS, ALU.mult, ALU.add))
                done()
                pool.tensor_tensor(rstd[:, :], mean[:, :], neghalf[:, :], ALU.pow).then_inc(rstd_ready, 1)

            row_scales(0, NB)

            pool.wait_ge(cs_kept, 2)
            pool.dma_start(cs_scratch, cst[:, :]).then_inc(cs_out, 16)
            pool.wait_ge(cs_out, 16)
            steps = st
            with pool.Fori(0, G) as g:
                steps.enter(g, 3)
                pool.wait_ge(ssd_done, g + 1)
                pool.wait_ge(conv_out, g + 5)
                pool.dma_start(dec[:, :, :, :].rearrange("q c h l -> q c (h l)"),
                               cs_scratch.rearrange("(c r) l -> c (r l)", c=TOK)[:, bass.ds(g * HG * P, HG * P)]
                               .rearrange("(o c) n -> o c n", o=1).broadcast_to([P, TOK, HG * P])
                               ).then_inc(dec_in, 16)
                pool.tensor_copy(chan[:, :, :], xc[:, bass.ds(g * BT, BT), :]).then_inc(group_in, 1)
                pool.tensor_copy(bg[:, :], bc[:, bass.ds(g, 1), :]).then_inc(group_in, 1)
                pool.tensor_copy(cg[:, :], bc[:, bass.ds(g + G, 1), :]).then_inc(group_in, 1)
                pool.wait_ge(dec_in, 16 * g + 16)
                pool.tensor_tensor(dec[:, :, :, :].rearrange("q c h l -> q (c h) l"),
                                   dec[:, :, :, :].rearrange("q c h l -> q (c h) l"),
                                   mask[:, :].rearrange("q (o l) -> q o l", o=1).broadcast_to([P, TOK * HG, P]),
                                   ALU.add).then_inc(dec_masked, 1)
                pool.wait_ge(x_kept, g + 1)
                pool.tensor_tensor(xdt[:, :, :, :], xs[:, :, :, :],
                                   dt_[:, :, bass.ds(g * HG, HG)].rearrange("q c (h o) -> q c h o", o=1)
                                   .broadcast_to([P, TOK, HG, HD]), ALU.mult).then_inc(xdt_done, 1)
                pool.wait_ge(xdt_done, g + 1)
                pool.tensor_tensor(xs[:, :, :, :], xs[:, :, :, :],
                                   skip[:, bass.ds(g * HG, HG)].rearrange("q (c h o) -> q c h o", o=1, c=1)
                                   .broadcast_to([P, TOK, HG, HD]), ALU.mult).then_inc(skip_done, 1)
                pool.wait_ge(g_squares, g + 1)
                step(pool.nop())
                step(pool.tensor_scalar(gmean[:, :], gsq[:, :], 1.0 / BLK, EPS, ALU.mult, ALU.add))
                done()
                step(pool.tensor_tensor(grstd[:, :], gmean[:, :], neghalf[:, :], ALU.pow))
                done()
                pool.nop().then_inc(g_rstd, 1)
            steps.leave(G)

            def keep_h(phase):
                u = UPDATE[phase]
                with pool.Fori(0, NB) as i:
                    pool.wait_ge(filled, FILL[phase] + i + 1)
                    pool.tensor_copy(block_of(h, i), stage[:, :, :]).then_inc(h_kept, 1)
                row_scales(u + 1, NB * (u + 2))

            keep_h("wout")
            pool.dma_start(prow[:, :, :], p[0, 0].rearrange("(t q) n -> q t n", q=P)).then_inc(p_in, 16)
            keep_h("down0")
            keep_h("ple0")
            pool.wait_ge(mm_done, CHUNK["ple0"])
            pool.wait_ge(turn, TURN["ple0"])
            step(pool.memset(mask3[:, :], 0.0))
            done()
            for n in (0, 2):
                step(pool.affine_select(out=mask3[:, n * P:(n + 1) * P], in_=mask3[:, n * P:(n + 1) * P],
                                        compare_op=ALU.is_ge, fill=NEG, base=0, pattern=[[-1, P]],
                                        channel_multiplier=1))
            done()
            pool.nop().then_inc(mask3_done, 1)
            keep_h("wo")
            pool.dma_start(prow[:, :, :], p[1, 0].rearrange("(t q) n -> q t n", q=P)).then_inc(p_in, 16)
            keep_h("down1")
            pool.dma_start(fgain[:, :], final_norm_g.rearrange("(o n) -> o n", o=1).broadcast_to([P, D])
                           ).then_inc(fgain_in, 16)
            keep_h("ple1")

        def split_slots(c, sizes):
            return [(c + n, n % RING, size) for n, size in enumerate(sizes)]

        @block.scalar
        def _(act):
            st = Steps()

            def hi(c, n, tiles=CK, uses=None):
                s = n % RING
                act.wait_ge(load[s], uses)
                if not (isinstance(c, int) and c < RING):
                    act.wait_ge(mm_done, c - RING + 1)
                nc.scalar.activation(wh[:, s, 0:tiles, :], raw[:, s, 0:tiles, :], ACT.Copy).then_inc(hi_done, 1)

            def hi_of(phase, i, m, first, last, sizes=None):
                for n in range(first, last):
                    c = CHUNK[phase] + i * m + n
                    uses = 16 * ((CHUNK[phase] + n) // RING + 1) + i * (16 * m // RING)
                    hi(c, n, sizes[n] if sizes and n < m else CK, uses)

            def turned_hi(t, dst, gain=None):
                act.wait_ge(turn, t + 1)
                apart(act)
                if gain is None:
                    nc.scalar.activation(dst, turned[:, :, :], ACT.Copy).then_inc(turn_act, 1)
                    return
                for k in range(BT):
                    ins = nc.scalar.activation(dst[:, k, :], turned[:, k, :], ACT.Copy, scale=gain(k))
                ins.then_inc(turn_act, 1)

            def gain_of(name, first):
                return lambda k: gains[:, bass.ds(GAIN[name] + first + k, 1)]

            act.wait_ge(gain_kept, 2)
            for b in range(NB):
                act.wait_ge(x_in[b], 16)
                for t in range(TOK):
                    if t or b:
                        act.wait_ge(act_step, st.last())
                    nc.scalar.activation(junk[:, :], h[:, t, b * BLK:(b + 1) * BLK], ACT.Square,
                                         accum_out=ssq[:, t, b:b + 1]).then_inc(act_step, 1)
                    st.next()
                act.wait_ge(act_step, st.last())
                act.nop().then_inc(squares, 1)
                turned_hi(b, uh[:, b * BT:(b + 1) * BT, :], gain_of("mix0", b * BT))
            act.wait_ge(dt_in, 16)
            nc.scalar.activation(dwh[:, :, :], draw[:, :, :], ACT.Copy).then_inc(dt_hi, 1)
            for n in range(AHEAD - 1):
                hi(n, n, CK, 16 * (n // RING + 1))
            act.wait_ge(bias_in, 48)
            nc.scalar.activation(nega[:, :], alog[:, :], ACT.Exp).then_inc(dt_act, 1)
            act.wait_ge(dt_x, 1)
            nc.scalar.activation(dabs[:, :], dx[:, :], ACT.Abs).then_inc(dt_act, 1)
            act.wait_ge(dt_act, 2)
            nc.scalar.activation(dexp[:, :], dabs[:, :], ACT.Exp, scale=-1.0).then_inc(dt_act, 1)
            nc.scalar.activation(drel[:, :], dx[:, :], ACT.Relu).then_inc(dt_act, 1)
            hi(AHEAD - 1, AHEAD - 1, CK, 32)

            m = len(full)

            def conv_job(i, out_tiles, tile0, t):
                hi_of("xbc", i, m, AHEAD, m + 3)
                hi_of("xbc", i, m, m + 3, m + AHEAD)
                act.wait_ge(turn, t + 1)
                apart(act)
                for k in range(BT):
                    ins = nc.scalar.activation(out_tiles[:, bass.ds(tile0 + k, 1), :], turned[:, k, :], ACT.Identity,
                                               bias=conv[:, CONV, bass.ds(wt(tile0, k, out_tiles), 1)],
                                               scale=conv[:, CONV - 1, bass.ds(wt(tile0, k, out_tiles), 1)]
                                               ).then_inc(conv_bias, 1)
                act.wait_ge(conv_bias, BT * (t - TURN["xbc"] + 1))
                act.nop().then_inc(turn_act, 1)
                act.wait_ge(conv_taps, t - TURN["xbc"] + 1)
                act.nop().then_inc(taps_seen, 1)
                part = out_tiles[:, bass.ds(tile0, BT), :]
                nc.scalar.activation(part, part, ACT.Silu).then_inc(conv_out, 1)

            def wt(tile0, k, out_tiles):
                return tile0 + k + (DI // P if out_tiles is bc else 0)

            with act.Fori(0, 4) as i:
                conv_job(i, bc, i * BT, TURN["xbc"] + i)
            with act.Fori(0, G) as i:
                conv_job(i + 4, xc, i * BT, TURN["xbc"] + 4 + i)

            act.wait_ge(cs_kept, 1)
            nc.scalar.activation(ecs[:, :], cs[:, 1, :], ACT.Exp).then_inc(ecs_done, 1)
            with act.Fori(0, G) as g:
                st.enter(g, 2)
                act.wait_ge(x_turn, g + 1)
                act.wait_ge(filled, FILL["z"] + g)
                nc.scalar.activation(xs[:, :, :, :].rearrange("q c h d -> q c (h d)"), py[:, :, :],
                                     ACT.Copy).then_inc(x_kept, 1)
                act.wait_ge(bg_turn, g + 1)
                nc.scalar.activation(btok[:, :], pg[:, TOK * P:(TOK + 1) * P], ACT.Copy).then_inc(b_kept, 1)
                act.wait_ge(diff_done, g + 1)
                nc.scalar.activation(dec[:, :, :, :], dec[:, :, :, :], ACT.Exp).then_inc(exp_done, 1)
                hi_of("z", g, m, AHEAD, m)
                act.wait_ge(st_mm, g + 1)
                nc.scalar.activation(state[:, :], pst[:, :], ACT.Copy).then_inc(st_kept, 1)
                hi_of("z", g, m, m, m + 3)
                act.wait_ge(turn, TURN["z"] + g)
                act.wait_ge(rstd_ready, 1)
                for t in range(TOK):
                    bank_ready(act, t, "z", g)
                    nc.scalar.activation(stage[:, t, :], acc[t][:, :], ACT.Silu, scale=rstd[:, t:t + 1]
                                         ).then_inc(act_step, 1)
                    st.next()
                    act.wait_ge(act_step, st.last())
                    act.nop().then_inc(acc_free[t], 1)
                act.nop().then_inc(gate_in, 1)
                act.wait_ge(gated, g + 1)
                for t in range(TOK):
                    nc.scalar.activation(junk[:, :], stage[:, t, :], ACT.Square, accum_out=gsq[:, t:t + 1]
                                         ).then_inc(g_squares_step, 1)
                    act.wait_ge(g_squares_step, 2 * g + t + 1)
                act.nop().then_inc(g_squares, 1)
                hi_of("z", g, m, m + 3, m + AHEAD)
                turned_hi(TURN["z"] + g, yt[:, bass.ds(g, 1), 0, :, :].rearrange("q o k n -> q (o k) n"),
                          lambda k: gains[:, bass.ds(GAIN["ssm"] + g * BT + k, 1)])
            st.leave(G)

            def sum_squares(phase, i, k):
                act.wait_ge(filled, FILL[phase] + i + 1)
                for t in range(TOK):
                    apart(act)
                    nc.scalar.activation(junk[:, :], stage[:, t, :], ACT.Square,
                                         accum_out=ssq[:, t, bass.ds(i, 1)]).then_inc(act_step, 1)
                    st.next()
                    act.wait_ge(act_step, st.last())
                act.nop().then_inc(squares, 1)

            def update(phase, sizes, dst, gain):
                m = len(sizes)
                with act.Fori(0, NB) as i:
                    st.enter(i, 2)
                    hi_of(phase, i, m, AHEAD, m + 3, sizes)
                    sum_squares(phase, i, 0)
                    hi_of(phase, i, m, m + 3, m + AHEAD)
                    turned_hi(TURN[phase] + i, dst[:, bass.ds(i * BT, BT), :],
                              lambda k: gains[:, bass.ds(GAIN[gain] + i * BT + k, 1)])
                st.leave(NB)

            def swiglu(l):
                m, name = len(full), f"gu{l}"
                with act.Fori(0, FB) as i:
                    st.enter(i, 2)
                    hi_of(name, 2 * i, m, AHEAD, m + 3)
                    act.wait_ge(turn, TURN[name] + i)
                    act.wait_ge(h_kept, NB * (UPDATE["wo" if l else "wout"] + 1))
                    act.wait_ge(rstd_ready, 5 if l else 2)
                    for t in range(TOK):
                        bank_ready(act, t, name, 2 * i)
                        nc.scalar.activation(stage[:, t, :], acc[t][:, :], ACT.Silu, scale=rstd[:, t:t + 1]
                                             ).then_inc(act_step, 1)
                        st.next()
                        act.wait_ge(act_step, st.last())
                        act.nop().then_inc(acc_free[t], 1)
                    act.nop().then_inc(gate_in, 1)
                    hi_of(name, 2 * i, m, m + 3, 2 * m + 3)
                    hi_of(name, 2 * i, m, 2 * m + 3, 2 * m + AHEAD)
                    turned_hi(TURN[name] + i, hh[:, bass.ds(i * BT, BT), :])
                st.leave(FB)

            def side_operand(l):
                act.wait_ge(p_turn, l + 1)
                nc.scalar.activation(ph[:, :, :].rearrange("q k n -> q (k n)"), pst[:, :], ACT.Copy).then_inc(p_hi, 1)

            def side(l):
                c = CHUNK[f"pp{l}"]
                for jb in range(2):
                    act.wait_ge(mm_done, c + 2 * jb + 2)
                    for t in range(TOK):
                        nc.scalar.activation(pp[:, t, (2 * jb + 1) * BLK:(2 * jb + 2) * BLK], py[:, t, :], ACT.Copy
                                             ).then_inc(act_step, 1)
                        st.next()
                    act.wait_ge(act_step, st.last())
                    act.nop().then_inc(side_kept, 1)
                    for n in range(AHEAD, AHEAD + 2):
                        cc = c + 2 * jb + n
                        hi(cc, cc, CK, 16 * (cc // RING + 1))

            def gate_update(l, i, dst=None, gain=None, last=False):
                m, name = len(full), f"ple{l}"
                if last:
                    hi_of(name, i, m, AHEAD, m)
                else:
                    hi_of(name, i, m, AHEAD, m + 3)
                act.wait_ge(turn, TURN["ple0"] + i if l == 0 else TURN["down1"] + NB)
                act.wait_ge(h_kept, NB * UPDATE[name] + i)
                act.wait_ge(rstd_ready, 3 + 3 * l)
                for t in range(TOK):
                    bank_ready(act, t, name, i)
                    nc.scalar.activation(stage[:, t, :], acc[t][:, :], ACT.Sigmoid, scale=rstd[:, t:t + 1]
                                         ).then_inc(act_step, 1)
                    st.next()
                    act.wait_ge(act_step, st.last())
                    act.nop().then_inc(acc_free[t], 1)
                act.nop().then_inc(gate_in, 1)
                sum_squares(name, i, 2)
                if not last:
                    hi_of(name, i, m, m + 3, m + AHEAD)
                if dst is not None:
                    turned_hi(TURN[name] + i, dst[:, bass.ds(i * BT, BT), :],
                              lambda k: gains[:, bass.ds(GAIN[gain] + i * BT + k, 1)])

            def exps(n, hd):
                act.wait_ge(s_top, n * BT + hd + 1)
                for q, (lo, up) in enumerate(((0, P), (P, 3 * P))):
                    nc.scalar.activation(sc[:, hd % 2, lo:up], sc[:, hd % 2, lo:up], ACT.Exp,
                                         bias=ntop[:, hd, q:q + 1], scale=SCALE,
                                         accum_out=den[:, hd, q:q + 1]).then_inc(s_exp, 1)

            def evac_scaled(phase, i, dst):
                for t in range(TOK):
                    bank_ready(act, t, phase, i)
                    apart(act)
                    nc.scalar.activation(dst[:, t, :], acc[t][:, :], ACT.Copy, scale=rstd[:, t:t + 1]
                                         ).then_inc(act_step, 1)
                    st.next()
                    act.wait_ge(act_step, st.last())
                    act.nop().then_inc(acc_free[t], 1)

            def half_turned(t, dst):
                act.wait_ge(turn, t + 1)
                nc.scalar.activation(dst[:, 0:2, :], turned[:, 0:2, :], ACT.Copy).then_inc(turn_act, 1)

            update("wout", inner, uh, "ffn0")
            swiglu(0)
            side_operand(0)
            update("down0", hidden, uh, "ple0")
            side(0)
            with act.Fori(0, NB) as i:
                st.enter(i, 4)
                gate_update(0, i, vh, "mix1")
            st.leave(NB)
            with act.Fori(0, NB) as i:
                st.enter(i, 2)
                hi_of("v", i, m, AHEAD, m + 3)
                act.wait_ge(rstd_ready, 4)
                evac_scaled("v", i, block_of(v, i))
                hi_of("v", i, m, m + 3, m + AHEAD)
            st.leave(NB)

            def qk_pair(j, attend):
                hi_of("qk", 2 * j, m, AHEAD, m)
                if attend:
                    exps(j - 1, 0)
                    exps(j - 1, 1)
                hi_of("qk", 2 * j, m, m, m + 2)
                if attend:
                    exps(j - 1, 2)
                hi_of("qk", 2 * j, m, m + 2, m + 3)
                if attend:
                    exps(j - 1, 3)
                if attend:
                    act.wait_ge(turn, TURN["qk"] + 3 * (j - 1) + 1)
                else:
                    act.wait_ge(turn, TURN["q0"])
                    act.wait_ge(h_kept, NB * (UPDATE["ple0"] + 1))
                evac_scaled("qk", 2 * j, stage)
                act.nop().then_inc(filled, 1)
                hi_of("qk", 2 * j, m, m + 3, m + AHEAD)
                tq = TURN["qk"] + 3 * (j - 1) + 1 if attend else TURN["q0"]
                if attend:
                    act.wait_ge(s_mm, BT * j)
                half_turned(tq, qt)
                hi_of("qk", 2 * j, m, m + AHEAD, 2 * m - (0 if attend else 0))
                if attend:
                    to = TURN["qk"] + 3 * (j - 1) + 2
                    turned_hi(to, oh[:, bass.ds((j - 1) * BT, BT), :])
                hi_of("qk", 2 * j, m, 2 * m, 2 * m + 3)
                act.wait_ge(turn, tq + 1)
                evac_scaled("qk", 2 * j + 1, stage)
                act.nop().then_inc(filled, 1)
                hi_of("qk", 2 * j, m, 2 * m + 3, 2 * m + AHEAD)
                tk = TURN["qk"] + 3 * j if attend else TURN["qk"]
                half_turned(tk, kt)

            st.enter(0, 0)
            qk_pair(0, False)
            st.leave(1)
            with act.Fori(1, NB) as j:
                st.base -= 4
                st.enter(j, 4)
                qk_pair(j, True)
            st.leave(NB)
            hi_of("wo", 0, m, AHEAD, AHEAD + 1)
            exps(NB - 1, 0)
            exps(NB - 1, 1)
            hi_of("wo", 0, m, AHEAD + 1, AHEAD + 2)
            exps(NB - 1, 2)
            exps(NB - 1, 3)
            hi_of("wo", 0, m, AHEAD + 2, m)
            turned_hi(TURN["o3"], oh[:, (NB - 1) * BT:NB * BT, :])

            def wo_rest(i):
                sum_squares("wo", i, 0)
                hi_of("wo", i, m, m + 3, m + AHEAD)
                turned_hi(TURN["wo"] + i, uh[:, bass.ds(i * BT, BT), :],
                          lambda k: gains[:, bass.ds(GAIN["ffn1"] + i * BT + k, 1)])

            hi_of("wo", 0, m, m, m + 3)
            wo_rest(0)
            with act.Fori(1, NB) as i:
                st.base -= 2
                st.enter(i, 2)
                hi_of("wo", i, m, AHEAD, m + 3)
                wo_rest(i)
            st.leave(NB)
            swiglu(1)
            side_operand(1)
            update("down1", hidden, uh, "ple1")
            side(1)
            with act.Fori(0, NB - 1) as i:
                st.enter(i, 4)
                gate_update(1, i)
            st.leave(NB - 1)
            gate_update(1, NB - 1, last=True)

        @block.vector
        def _(dve):
            st = Steps()

            def lo(c, n, tiles=CK):
                s = n % RING
                dve.wait_ge(hi_done, c + 1)
                nc.vector.tensor_tensor(wl[:, s, 0:tiles, :], raw[:, s, 0:tiles, :],
                                        wh[:, s, 0:tiles, :].bitcast(F32), ALU.subtract).then_inc(lo_done, 1)

            def lo_of(phase, i, m, first, last, sizes=None):
                for n in range(first, last):
                    lo(CHUNK[phase] + i * m + n, n, sizes[n] if sizes and n < m else CK)

            def turned_lo(t, dst, high, gain=None):
                dve.wait_ge(turn_act, t + 1)
                if gain is None:
                    nc.vector.tensor_tensor(dst, turned[:, :, :], high.bitcast(F32), ALU.subtract
                                            ).then_inc(turn_dve, 1)
                    return
                for k in range(BT):
                    ins = nc.vector.scalar_tensor_tensor(out=dst[:, k, :], in0=turned[:, k, :], scalar=gain(k),
                                                         in1=high[:, k, :].bitcast(F32), op0=ALU.mult,
                                                         op1=ALU.subtract)
                ins.then_inc(turn_dve, 1)

            def step(ins):
                ins.then_inc(dve_step, 1)
                st.next()

            def done(back=0):
                dve.wait_ge(dve_step, st.last(back))

            dve.wait_ge(gain_turn, 1)
            nc.vector.tensor_copy(gains[:, :], acc[0][:, 0:P]).then_inc(gain_kept, 1)
            dve.wait_ge(gain_turn, 2)
            nc.vector.tensor_copy(conv[:, :, :].rearrange("q j k -> q (j k)"), acc[1][:, 0:(CONV + 1) * CT]
                                  ).then_inc(gain_kept, 1)
            dve.wait_ge(gain_kept, 2)
            dve.nop().then_inc(acc_free[0], 1)
            dve.nop().then_inc(acc_free[1], 1)
            dve.nop().then_inc(pg_free, 1)
            for b in range(NB):
                turned_lo(b, ul[:, b * BT:(b + 1) * BT, :], uh[:, b * BT:(b + 1) * BT, :],
                          lambda k: gains[:, GAIN["mix0"] + b * BT + k:GAIN["mix0"] + b * BT + k + 1])
            dve.wait_ge(dt_hi, 1)
            nc.vector.tensor_tensor(dwl[:, :, :], draw[:, :, :], dwh[:, :, :].bitcast(F32), ALU.subtract
                                    ).then_inc(dt_lo, 1)
            for n in range(AHEAD - 1):
                lo(n, n)
            dve.wait_ge(dt_mm, 1)
            dve.wait_ge(bias_in, 48)
            dve.wait_ge(rstd_ready, 1)
            for t in range(TOK):
                step(nc.vector.scalar_tensor_tensor(out=dx[:, t * SH:(t + 1) * SH], in0=py[:, 0, t * SH:(t + 1) * SH],
                                                    scalar=rstd[:, t:t + 1], in1=dtb[:, :], op0=ALU.mult, op1=ALU.add))
            done()
            dve.nop().then_inc(dt_x, 1)
            dve.nop().then_inc(y_taken, 1)
            dve.wait_ge(dt_act, 4)
            step(nc.vector.tensor_scalar(dden[:, :], dexp[:, :], 2.0, None, ALU.add))
            done()
            step(nc.vector.reciprocal(drec[:, :], dden[:, :]))
            done()
            step(nc.vector.tensor_tensor(dy[:, :], dexp[:, :], drec[:, :], ALU.mult))
            done()
            step(nc.vector.tensor_tensor(dy2[:, :], dy[:, :], dy[:, :], ALU.mult))
            done()
            step(nc.vector.tensor_scalar(dq[0][:, :], dy2[:, :], 1.0 / 17, None, ALU.mult))
            done()
            for n, term in enumerate((15, 13, 11, 9, 7, 5, 3)):
                step(nc.vector.scalar_tensor_tensor(out=dq[1 - n % 2][:, :], in0=dq[n % 2][:, :], scalar=1.0 / term,
                                                    in1=dy2[:, :], op0=ALU.add, op1=ALU.mult))
                done()
            step(nc.vector.scalar_tensor_tensor(out=dq[0][:, :], in0=dq[1][:, :], scalar=1.0, in1=dy[:, :],
                                                op0=ALU.add, op1=ALU.mult))
            done()
            step(nc.vector.scalar_tensor_tensor(out=dt_[:, :, :].rearrange("q t h -> q (t h)"), in0=dq[0][:, :],
                                                scalar=2.0, in1=drel[:, :], op0=ALU.mult, op1=ALU.add))
            done()
            for t in range(TOK):
                step(nc.vector.scalar_tensor_tensor(out=dta[:, t, :], in0=dt_[:, t, :], scalar=-1.0, in1=nega[:, :],
                                                    op0=ALU.mult, op1=ALU.mult))
            done()
            dve.nop().then_inc(dta_done, 1)
            lo(AHEAD - 1, AHEAD - 1)
            m = len(full)

            def conv_job(i, out_tiles, tile0, t, cs_here=False):
                st0 = 0
                lo_of("xbc", i, m, AHEAD, m)
                if cs_here:
                    dve.wait_ge(cs_mm, 1)
                    step(nc.vector.tensor_copy(cs[:, :, :].rearrange("q t h -> q (t h)"), py[:, 1, 0:TOK * SH]))
                    done()
                    dve.nop().then_inc(cs_kept, 1)
                    dve.wait_ge(cs_mm, 2)
                    step(nc.vector.tensor_copy(cst[:, :], py[:, 1, TOK * SH:TOK * SH + P]))
                    done()
                    dve.nop().then_inc(cs_kept, 1)
                lo_of("xbc", i, m, m, m + 3)
                dve.wait_ge(turn, t)
                dve.wait_ge(rstd_ready, 1)
                for a in range(TOK):
                    bank_ready(dve, a, "xbc", i)
                    step(nc.vector.tensor_scalar(stage[:, a, :], acc[a][:, :], rstd[:, a:a + 1], None, ALU.mult))
                    done()
                    dve.nop().then_inc(acc_free[a], 1)
                dve.nop().then_inc(filled, 1)
                lo_of("xbc", i, m, m + 3, m + AHEAD)
                n = TOK * P
                for tap in range(CONV - 2, -1, -1):
                    back = CONV - 1 - tap
                    for k in range(BT):
                        if back == 1:
                            dve.wait_ge(conv_bias, BT * (t - TURN["xbc"] + 1))
                        else:
                            done(BT - 1)
                        o = out_tiles[:, bass.ds(tile0 + k, 1), back:n]
                        wk = tile0 + k + (DI // P if out_tiles is bc else 0)
                        step(nc.vector.scalar_tensor_tensor(out=o, in0=turned[:, k:k + 1, 0:n - back],
                                                            scalar=conv[:, tap, bass.ds(wk, 1)], in1=o,
                                                            op0=ALU.mult, op1=ALU.add))
                done()
                dve.nop().then_inc(turn_dve, 1)
                dve.nop().then_inc(conv_taps, 1)

            conv_job(0, bc, 0, TURN["xbc"], cs_here=True)
            with dve.Fori(1, 4) as i:
                st.base -= 14
                st.enter(i, 14)
                conv_job(i, bc, i * BT, TURN["xbc"] + i)
            st.leave(4)
            with dve.Fori(0, G) as i:
                st.enter(i, 14)
                conv_job(i + 4, xc, i * BT, TURN["xbc"] + 4 + i)
            st.leave(G)

            with dve.Fori(0, G) as g:
                st.enter(g, 8)
                dve.wait_ge(dec_masked, g + 1)
                for c in range(TOK):
                    ins = nc.vector.tensor_tensor(dec[:, c, :, :], dec[:, c, :, :],
                                                  cs[:, c, bass.ds(g * HG, HG)].rearrange("q (h o) -> q h o", o=1)
                                                  .broadcast_to([P, HG, P]), ALU.subtract)
                    step(ins)
                done()
                dve.nop().then_inc(diff_done, 1)
                lo_of("z", g, m, AHEAD, AHEAD + 1)
                dve.wait_ge(exp_done, g + 1)
                dve.wait_ge(xdt_done, g + 1)
                nc.vector.tensor_tensor(xw[:, :, :], xdt[:, 0, :, :],
                                        dec[:, 0, :, P - 1:P].broadcast_to([P, HG, HD]), ALU.mult
                                        ).then_inc(xw_done, 1)
                dve.wait_ge(xw_done, g + 1)
                dve.wait_ge(bg_turn, g + 1)
                for c in range(TOK):
                    step(nc.vector.tensor_tensor(dec[:, c, :, :], dec[:, c, :, :],
                                                 pg[:, c * P:(c + 1) * P].rearrange("q (o l) -> q o l", o=1)
                                                 .broadcast_to([P, HG, P]), ALU.mult))
                done()
                dve.nop().then_inc(m_done, 1)
                dve.nop().then_inc(pg_free, 1)
                lo_of("z", g, m, AHEAD + 1, m + 3)
                dve.wait_ge(ssd_done, g + 2)
                dve.wait_ge(skip_done, g + 1)
                step(nc.vector.tensor_tensor(xs[:, :, :, :].rearrange("q c h d -> q c (h d)"),
                                             xs[:, :, :, :].rearrange("q c h d -> q c (h d)"), py[:, :, :], ALU.add))
                dve.wait_ge(ecs_done, 1)
                step(nc.vector.tensor_tensor(xw[:, :, :], pst[:, :].rearrange("q (h d) -> q h d", h=HG),
                                             ecs[:, bass.ds(g * HG, HG)].rearrange("q (h o) -> q h o", o=1)
                                             .broadcast_to([P, HG, HD]), ALU.mult))
                done()
                dve.nop().then_inc(y_taken, 1)
                step(nc.vector.tensor_tensor(xs[:, 1, :, :], xs[:, 1, :, :], xw[:, :, :], ALU.add))
                done()
                dve.wait_ge(gate_in, g + 1)
                nc.vector.tensor_tensor(stage[:, :, :], stage[:, :, :],
                                        xs[:, :, :, :].rearrange("q c h d -> q c (h d)"), ALU.mult).then_inc(gated, 1)
                dve.wait_ge(g_rstd, g + 1)
                for t in range(TOK):
                    ins = nc.vector.tensor_scalar(stage[:, t, :], stage[:, t, :], grstd[:, t:t + 1], None, ALU.mult)
                    if t == 0:
                        step(ins)
                done()
                ins.then_inc(filled, 1)
                lo_of("z", g, m, m + 3, m + AHEAD)
                turned_lo(TURN["z"] + g, yt[:, bass.ds(g, 1), 1, :, :].rearrange("q o k n -> q (o k) n"),
                          yt[:, bass.ds(g, 1), 0, :, :].rearrange("q o k n -> q (o k) n"),
                          lambda k: gains[:, bass.ds(GAIN["ssm"] + g * BT + k, 1)])
            st.leave(G)

            def add_block(phase, i):
                for t in range(TOK):
                    bank_ready(dve, t, phase, i)
                    step(nc.vector.tensor_tensor(stage[:, t, :], acc[t][:, :], h[:, t, bass.ds(i * BLK, BLK)], ALU.add))
                    done()
                    dve.nop().then_inc(acc_free[t], 1)
                dve.nop().then_inc(filled, 1)

            def stage_free(phase, i):
                dve.wait_ge(turn, TURN[phase] + i)
                if UPDATE[phase]:
                    dve.wait_ge(h_kept, NB * UPDATE[phase] + i)
                dve.wait_ge(squares, NB * (UPDATE[phase] + 1) + i)

            def update(phase, sizes, dst, high, gain, i=None):
                m = len(sizes)
                with dve.Fori(0, NB) as i:
                    st.enter(i, 2)
                    lo_of(phase, i, m, AHEAD, m + 3, sizes)
                    dve.wait_ge(turn, TURN[phase] + i)
                    if UPDATE[phase]:
                        dve.wait_ge(h_kept, NB * UPDATE[phase] + i)
                    dve.wait_ge(squares, NB * (UPDATE[phase] + 1) + i)
                    if not UPDATE[phase]:
                        dve.wait_ge(rstd_ready, 1)
                    add_block(phase, i)
                    lo_of(phase, i, m, m + 3, m + AHEAD)
                    turned_lo(TURN[phase] + i, dst[:, bass.ds(i * BT, BT), :], high[:, bass.ds(i * BT, BT), :],
                              lambda k: gains[:, bass.ds(GAIN[gain] + i * BT + k, 1)])
                    if not UPDATE[phase]:
                        dve.wait_ge(h_kept, i + 1)
                st.leave(NB)

            def swiglu(l):
                m, name = len(full), f"gu{l}"
                with dve.Fori(0, FB) as i:
                    st.enter(i, 2)
                    lo_of(name, 2 * i, m, AHEAD, 2 * m + 3)
                    dve.wait_ge(gate_in, G + (FB + NB) * l + i + 1)
                    for t in range(TOK):
                        bank_ready(dve, t, name, 2 * i + 1)
                        step(nc.vector.scalar_tensor_tensor(out=stage[:, t, :], in0=acc[t][:, :],
                                                            scalar=rstd[:, t:t + 1], in1=stage[:, t, :],
                                                            op0=ALU.mult, op1=ALU.mult))
                        done()
                        dve.nop().then_inc(acc_free[t], 1)
                    dve.nop().then_inc(filled, 1)
                    lo_of(name, 2 * i, m, 2 * m + 3, 2 * m + AHEAD)
                    turned_lo(TURN[name] + i, hl[:, bass.ds(i * BT, BT), :], hh[:, bass.ds(i * BT, BT), :])
                st.leave(FB)

            def side_operand(l):
                dve.wait_ge(p_hi, l + 1)
                nc.vector.tensor_tensor(pl[:, :, :].rearrange("q k n -> q (k n)"), pst[:, :],
                                        ph[:, :, :].rearrange("q k n -> q (k n)").bitcast(F32), ALU.subtract
                                        ).then_inc(p_lo, 1)

            def side(l):
                c = CHUNK[f"pp{l}"]
                for jb in range(2):
                    for t in range(TOK):
                        bank_ready(dve, t, f"pp{l}", jb)
                        step(nc.vector.tensor_copy(pp[:, t, 2 * jb * BLK:(2 * jb + 1) * BLK], acc[t][:, :]))
                        done()
                        dve.nop().then_inc(acc_free[t], 1)
                    for n in range(AHEAD, AHEAD + 2):
                        lo(c + 2 * jb + n, c + 2 * jb + n)

            def gate_update(l, i, dst=None, high=None, gain=None, last=False):
                m, name = len(full), f"ple{l}"
                if last:
                    lo_of(name, i, m, AHEAD, m)
                else:
                    lo_of(name, i, m, AHEAD, m + 3)
                dve.wait_ge(gate_in, G + FB + (FB + NB) * l + i + 1)
                dve.wait_ge(side_kept, 2 * l + 2)
                step(nc.vector.tensor_tensor(stage[:, :, :], stage[:, :, :], block_of(pp, i), ALU.mult))
                done()
                nc.vector.tensor_tensor(stage[:, :, :], stage[:, :, :], block_of(h, i), ALU.add).then_inc(filled, 1)
                if not last:
                    lo_of(name, i, m, m + 3, m + AHEAD)
                if dst is not None:
                    turned_lo(TURN[name] + i, dst[:, bass.ds(i * BT, BT), :], high[:, bass.ds(i * BT, BT), :],
                              lambda k: gains[:, bass.ds(GAIN[gain] + i * BT + k, 1)])

            def tops(n, hd):
                b = hd % 2
                dve.wait_ge(s_mm, n * BT + hd + 1)
                dve.wait_ge(mask3_done, 1)
                src = (pg, pst)[b]
                if hd >= 2:
                    dve.wait_ge(pr_turn, n * BT + hd - 1)
                step(nc.vector.tensor_tensor(sc[:, b, :], src[:, 0:3 * P], mask3[:, :], ALU.add))
                done()
                for q, (lo_, up) in enumerate(((0, P), (P, 3 * P))):
                    step(nc.vector.tensor_reduce(top[:, hd, q:q + 1], sc[:, b, lo_:up], AX.X, ALU.max))
                done()
                nc.vector.tensor_scalar(ntop[:, hd, :], top[:, hd, :], -SCALE, None, ALU.mult).then_inc(s_top, 1)

            def probs(n, hd):
                dve.wait_ge(pr_turn, n * BT + hd + 1)
                if hd >= 2:
                    dve.wait_ge(o_mm, n * BT + hd - 1)
                nc.vector.tensor_copy(prt[:, hd % 2, :, :].rearrange("q k n -> q (k n)"), py[:, 0, 0:3 * P]
                                      ).then_inc(pr_kept, 1)

            def heads_out(n, hd):
                dve.wait_ge(s_exp, 2 * (n * BT + hd) + 2)
                step(nc.vector.reciprocal(rden[:, hd, :], den[:, hd, :]))
                done()
                dve.wait_ge(o_mm, n * BT + hd + 1)
                for q in range(TOK):
                    ins = nc.vector.tensor_scalar(orow[:, q, hd * P:(hd + 1) * P],
                                                  py[:, 1, (2 * (hd % 2) + q) * P:(2 * (hd % 2) + q + 1) * P],
                                                  rden[:, hd, q:q + 1], None, ALU.mult)
                    step(ins)
                done()
                dve.nop().then_inc(o_kept, 1)

            def half_turned(t, dst):
                dve.wait_ge(turn, t + 1)
                nc.vector.tensor_copy(dst[:, 2:4, :], turned[:, 2:4, :]).then_inc(turn_dve, 1)

            update("wout", inner, ul, uh, "ffn0")
            swiglu(0)
            side_operand(0)
            update("down0", hidden, ul, uh, "ple0")
            side(0)
            with dve.Fori(0, NB) as i:
                st.enter(i, 1)
                gate_update(0, i, vl, vh, "mix1")
            st.leave(NB)
            with dve.Fori(0, NB) as i:
                lo_of("v", i, m, AHEAD, m + AHEAD)

            STEPS = 24

            def qk_pair(j, attend):
                lo_of("qk", 2 * j, m, AHEAD, m)
                if attend:
                    tops(j - 1, 0)
                    tops(j - 1, 1)
                lo_of("qk", 2 * j, m, m, m + 2)
                if attend:
                    probs(j - 1, 0)
                    tops(j - 1, 2)
                lo_of("qk", 2 * j, m, m + 2, m + 3)
                if attend:
                    probs(j - 1, 1)
                    tops(j - 1, 3)
                    heads_out(j - 1, 0)
                    probs(j - 1, 2)
                    heads_out(j - 1, 1)
                lo_of("qk", 2 * j, m, m + 3, m + 4)
                if attend:
                    probs(j - 1, 3)
                    heads_out(j - 1, 2)
                lo_of("qk", 2 * j, m, m + 4, m + AHEAD)
                if attend:
                    heads_out(j - 1, 3)
                tq = TURN["qk"] + 3 * (j - 1) + 1 if attend else TURN["q0"]
                half_turned(tq, qt)
                lo_of("qk", 2 * j, m, m + AHEAD, 2 * m)
                if attend:
                    turned_lo(TURN["qk"] + 3 * (j - 1) + 2, ol[:, bass.ds((j - 1) * BT, BT), :],
                              oh[:, bass.ds((j - 1) * BT, BT), :])
                lo_of("qk", 2 * j, m, 2 * m, 2 * m + AHEAD)
                half_turned(TURN["qk"] + 3 * j if attend else TURN["qk"], kt)

            qk_pair(0, False)
            with dve.Fori(1, NB) as j:
                st.base -= STEPS
                st.enter(j, STEPS)
                qk_pair(j, True)
            st.leave(NB)
            n = NB - 1
            lo_of("wo", 0, m, AHEAD, AHEAD + 1)
            tops(n, 0)
            tops(n, 1)
            lo_of("wo", 0, m, AHEAD + 1, AHEAD + 2)
            probs(n, 0)
            tops(n, 2)
            probs(n, 1)
            tops(n, 3)
            heads_out(n, 0)
            probs(n, 2)
            heads_out(n, 1)
            probs(n, 3)
            heads_out(n, 2)
            heads_out(n, 3)
            lo_of("wo", 0, m, AHEAD + 2, m)
            turned_lo(TURN["o3"], ol[:, n * BT:(n + 1) * BT, :], oh[:, n * BT:(n + 1) * BT, :])

            def wo_rest(i):
                dve.wait_ge(turn, TURN["wo"] + i)
                dve.wait_ge(squares, NB * (UPDATE["wo"] + 1) + i)
                dve.wait_ge(h_kept, NB * UPDATE["wo"] + i)
                add_block("wo", i)
                lo_of("wo", i, m, m + 3, m + AHEAD)
                turned_lo(TURN["wo"] + i, ul[:, bass.ds(i * BT, BT), :], uh[:, bass.ds(i * BT, BT), :],
                          lambda k: gains[:, bass.ds(GAIN["ffn1"] + i * BT + k, 1)])

            lo_of("wo", 0, m, m, m + 3)
            wo_rest(0)
            with dve.Fori(1, NB) as i:
                st.base -= 2
                st.enter(i, 2)
                lo_of("wo", i, m, AHEAD, m + 3)
                wo_rest(i)
            st.leave(NB)
            swiglu(1)
            side_operand(1)
            update("down1", hidden, ul, uh, "ple1")
            side(1)
            with dve.Fori(0, NB - 1) as i:
                st.enter(i, 1)
                gate_update(1, i)
            st.leave(NB - 1)
            gate_update(1, NB - 1, last=True)
            dve.wait_ge(rstd_ready, 7)
            dve.wait_ge(h_kept, NB * 6)
            dve.wait_ge(fgain_in, 16)
            for b in range(NB):
                for t in range(TOK):
                    o = h[:, t, b * BLK:(b + 1) * BLK]
                    step(nc.vector.scalar_tensor_tensor(out=o, in0=o, scalar=rstd[:, t:t + 1],
                                                        in1=fgain[:, b * BLK:(b + 1) * BLK], op0=ALU.mult,
                                                        op1=ALU.mult))
                done()
                dve.nop().then_inc(out_ready, 1)

        @block.tensor
        def _(pe):
            def products(s, tiles, k, ah, al, banks, c, start, stop, job_=None):
                pe.wait_ge(lo_done, c + 1)
                for t in range(TOK):
                    if start and job_ is not None:
                        pe.wait_ge(acc_free[t], job_ + 1)
                    for n in range(tiles):
                        a, b = ah(k + n, t), al(k + n, t)
                        nc.tensor.matmul(banks[t], a, wh[:, s, n, :], start=start and n == 0, stop=False)
                        nc.tensor.matmul(banks[t], a, wl[:, s, n, :], start=False, stop=False)
                        ins = nc.tensor.matmul(banks[t], b, wh[:, s, n, :], start=False, stop=stop and n == tiles - 1)
                    if t == 0 and stop and job_ is not None:
                        ins.then_inc(acc_done, 1)
                ins.then_inc(mm_done, 1)

            def operand(high, low):
                return (lambda k, t: high[:, k, t * P:(t + 1) * P]), (lambda k, t: low[:, k, t * P:(t + 1) * P])

            banks = [acc[0][:, :], acc[1][:, :]]

            def job(phase, i, sizes, op, between=None):
                m, k = len(sizes), 0
                for n, size in enumerate(sizes):
                    c = CHUNK[phase] + i * m + n
                    products(n % RING, size, k, *op, banks, c, n == 0, n == m - 1, JOB[phase] + i)
                    k += size
                    if between and n in between:
                        between[n]()

            def turn_stage(t, src=None, wait=None):
                src = src or (lambda a, k: stage[:, a, k * P:(k + 1) * P])
                if wait:
                    wait()
                if not (isinstance(t, int) and t == 0):
                    pe.wait_ge(turn_act, t)
                    pe.wait_ge(turn_dve, t)
                for k in range(BT):
                    for a in range(TOK):
                        ins = nc.tensor.transpose(turned[:, k, a * P:(a + 1) * P], src(a, k), ident[:, :])
                ins.then_inc(turn, 1)

            def turn_fill(t, fill):
                return lambda: turn_stage(t, wait=lambda: pe.wait_ge(filled, fill + 1))

            pe.wait_ge(consts, 1)
            pe.wait_ge(small_in, 6 * 16)
            nc.tensor.transpose(acc[0][:, 0:P], grows[:, :], ident[:, :]).then_inc(gain_turn, 1)
            for n in range(CONV + 1):
                ins = nc.tensor.transpose(acc[1][:, n * CT:(n + 1) * CT], crows[:, n, :], ident[0:CT, 0:CT])
            ins.then_inc(gain_turn, 1)
            for b in range(NB):
                turn_stage(b, src=lambda a, k: h[:, a, b * BLK + k * P:b * BLK + (k + 1) * P],
                           wait=lambda: pe.wait_ge(x_in[b], 16))
            u = operand(uh, ul)
            pe.wait_ge(turn_dve, NB)
            pe.wait_ge(dt_lo, 1)
            for t in range(TOK):
                for k in range(KD):
                    o = py[:, 0, t * SH:(t + 1) * SH]
                    nc.tensor.matmul(o, u[0](k, t), dwh[:, k, :], start=k == 0, stop=False)
                    nc.tensor.matmul(o, u[0](k, t), dwl[:, k, :], start=False, stop=False)
                    ins = nc.tensor.matmul(o, u[1](k, t), dwh[:, k, :], start=False, stop=k == KD - 1)
            ins.then_inc(dt_mm, 1)

            def running_sums():
                pe.wait_ge(dta_done, 1)
                nc.tensor.matmul(py[:, 1, 0:TOK * SH], upper[:, :], dta[:, :, :].rearrange("q t h -> q (t h)"),
                                 start=True, stop=True).then_inc(cs_mm, 1)

            def turn_sums():
                pe.wait_ge(cs_kept, 1)
                nc.tensor.transpose(py[:, 1, TOK * SH:TOK * SH + P], cs[:, :, :].rearrange("q t h -> q (t h)"),
                                    ident[:, :]).then_inc(cs_mm, 1)

            job("xbc", 0, full, u, {3: running_sums, 6: turn_sums})
            pe.nop().then_inc(ssd_done, 1)
            with pe.Fori(1, CH // BLK) as i:
                job("xbc", i, full, u, {1: turn_fill(TURN["xbc"] - 1 + i, FILL["xbc"] - 1 + i)})

            pe.wait_ge(cs_kept, 2)
            with pe.Fori(0, G) as g:
                def group_turns():
                    pe.wait_ge(group_in, 3 * g + 3)
                    pe.wait_ge(y_taken, g + 1)
                    for a in range(TOK):
                        for k in range(BT):
                            ins = nc.tensor.transpose(py[:, a, k * P:(k + 1) * P], chan[:, k, a * P:(a + 1) * P],
                                                      ident[:, :])
                    ins.then_inc(x_turn, 1)
                    pe.wait_ge(pg_free, g + 1)
                    for a in range(TOK):
                        nc.tensor.matmul(pg[:, a * P:(a + 1) * P], bg[:, a * P:(a + 1) * P], cg[:, a * P:(a + 1) * P],
                                         start=True, stop=True)
                    nc.tensor.transpose(pg[:, TOK * P:(TOK + 1) * P], bg[:, 0:P], ident[:, :]).then_inc(bg_turn, 1)

                def chunk_state():
                    pe.wait_ge(xw_done, g + 1)
                    pe.wait_ge(b_kept, g + 1)
                    nc.tensor.matmul(pst[:, :], btok[:, :], xw[:, :, :].rearrange("q h d -> q (h d)"),
                                     start=True, stop=True).then_inc(st_mm, 1)

                def outputs():
                    pe.wait_ge(st_kept, g + 1)
                    nc.tensor.matmul(pst[:, :], cg[:, P:2 * P], state[:, :], start=True, stop=True)
                    pe.wait_ge(m_done, g + 1)
                    pe.wait_ge(x_kept, g + 1)
                    for a in range(TOK):
                        for hd in range(HG):
                            ins = nc.tensor.matmul(py[:, a, hd * HD:(hd + 1) * HD], dec[:, a, hd, :],
                                                   xdt[:, a, hd, :], start=True, stop=True)
                    ins.then_inc(ssd_done, 1)

                job("z", g, full, u, {0: group_turns, 2: turn_fill(TURN["z"] - 1 + g, FILL["z"] - 1 + g),
                                      4: chunk_state, 6: outputs})

            y = ((lambda k, t: yt[:, k // BT, 0, k % BT, t * P:(t + 1) * P]),
                 (lambda k, t: yt[:, k // BT, 1, k % BT, t * P:(t + 1) * P]))

            def operand_ready(t):
                pe.wait_ge(turn_dve, t)

            def lagged(phase, i, sizes, op, ready):
                job(phase, i, sizes, op, {1: turn_fill(TURN[phase] - 1 + i, FILL[phase] - 1 + i), 3: ready})

            with pe.Fori(0, NB) as i:
                lagged("wout", i, inner, y, lambda: pe.wait_ge(turn_dve, TURN["wout"] + i))

            def swiglu(l):
                name = f"gu{l}"
                with pe.Fori(0, FB) as i:
                    job(name, 2 * i, full, u, {1: turn_fill(TURN[name] - 1 + i, FILL[name] - 1 + i),
                                               5: lambda: pe.wait_ge(turn_dve, TURN[name] + i)})
                    job(name, 2 * i + 1, full, u)

            def down(l):
                name = f"down{l}"
                with pe.Fori(0, NB) as i:
                    job(name, i, hidden, operand(hh, hl), {1: turn_fill(TURN[name] - 1 + i, FILL[name] - 1 + i),
                                                           7: lambda: pe.wait_ge(turn_dve, TURN[name] + i)})

            def side_operand(l):
                pe.wait_ge(p_in, 16 * (l + 1))
                for k in range(KP):
                    for a in range(TOK):
                        ins = nc.tensor.transpose(pst[:, (k * TOK + a) * P:(k * TOK + a + 1) * P],
                                                  prow[:, a, k * P:(k + 1) * P], ident[:, :])
                ins.then_inc(p_turn, 1)

            def side(l):
                pe.wait_ge(p_lo, l + 1)
                op = operand(ph, pl)
                for jb in range(2):
                    c = CHUNK[f"pp{l}"] + 2 * jb
                    products(c % RING, CK, 0, *op, banks, c, True, True, JOB[f"pp{l}"] + jb)
                    if jb:
                        pe.wait_ge(side_kept, 2 * l + 1)
                    products((c + 1) % RING, CK, 0, *op, [py[:, 0, :], py[:, 1, :]], c + 1, True, True)
                    if jb == 0:
                        t = TURN[f"down{l}"] + NB
                        turn_stage(t - 1, wait=lambda: pe.wait_ge(filled, FILL[f"down{l}"] + NB))
                pe.wait_ge(turn_dve, t)

            swiglu(0)
            side_operand(0)
            down(0)
            side(0)
            uv = operand(vh, vl)
            job("ple0", 0, full, u)
            with pe.Fori(1, NB) as i:
                job("ple0", i, full, u, {1: turn_fill(TURN["ple0"] - 1 + i, FILL["ple0"] - 1 + i)})
            job("v", 0, full, uv, {1: turn_fill(TURN["ple0"] + NB - 1, FILL["ple0"] + NB - 1),
                                   5: lambda: pe.wait_ge(turn_dve, TURN["ple0"] + NB)})
            with pe.Fori(1, NB) as i:
                job("v", i, full, uv)

            def scores(n, hd):
                def _():
                    if hd >= 2:
                        pe.wait_ge(s_top, n * BT + hd - 1)
                    if hd == 0:
                        pe.wait_ge(turn_act, TURN["qk"] + 3 * n + 1)
                        pe.wait_ge(turn_dve, TURN["qk"] + 3 * n + 1)
                    o = (pg, pst)[hd % 2]
                    nc.tensor.matmul(o[:, 0:P], qt[:, hd, 0:P], kt[:, hd, 0:P], start=True, stop=True)
                    nc.tensor.matmul(o[:, P:3 * P], qt[:, hd, P:2 * P], kt[:, hd, :], start=True, stop=True
                                     ).then_inc(s_mm, 1)
                return _

            def turn_probs(n, hd):
                def _():
                    pe.wait_ge(s_exp, 2 * (n * BT + hd) + 2)
                    if hd:
                        pe.wait_ge(pr_kept, n * BT + hd)
                    for k in range(3):
                        ins = nc.tensor.transpose(py[:, 0, k * P:(k + 1) * P], sc[:, hd % 2, k * P:(k + 1) * P],
                                                  ident[:, :])
                    ins.then_inc(pr_turn, 1)
                return _

            def rows(n, hd):
                def _():
                    pe.wait_ge(pr_kept, n * BT + hd + 1)
                    if hd:
                        pe.wait_ge(o_kept, n * BT + hd)
                    o = py[:, 1, 2 * (hd % 2) * P:(2 * (hd % 2) + 2) * P]
                    col = bass.ds((n * BT + hd) * P, P)
                    nc.tensor.matmul(o[:, 0:P], prt[:, hd % 2, 0, :], v[:, 0, col], start=True, stop=True)
                    nc.tensor.matmul(o[:, P:2 * P], prt[:, hd % 2, 1, :], v[:, 0, col], start=True, stop=False)
                    nc.tensor.matmul(o[:, P:2 * P], prt[:, hd % 2, 2, :], v[:, 1, col], start=False, stop=True
                                     ).then_inc(o_mm, 1)
                return _

            def turn_out(n, t):
                return lambda: turn_stage(t, src=lambda a, k: orow[:, a, k * P:(k + 1) * P],
                                          wait=lambda: pe.wait_ge(o_kept, n * BT + BT))

            def then(*fs):
                def _():
                    for f in fs:
                        f()
                return _

            job("qk", 0, full, uv)
            job("qk", 1, full, uv, {1: turn_fill(TURN["q0"], FILL["qk"])})
            with pe.Fori(1, NB) as j:
                n = j - 1
                t = TURN["qk"] + 3 * (j - 1)
                job("qk", 2 * j, full, uv, {1: turn_fill(t, FILL["qk"] + 2 * j - 1),
                                            3: then(scores(n, 0), scores(n, 1)),
                                            5: then(turn_probs(n, 0), scores(n, 2)),
                                            6: then(turn_probs(n, 1), scores(n, 3), rows(n, 0)),
                                            7: then(turn_probs(n, 2), rows(n, 1))})
                job("qk", 2 * j + 1, full, uv, {0: then(turn_probs(n, 3), rows(n, 2)),
                                                1: then(rows(n, 3), turn_fill(t + 1, FILL["qk"] + 2 * j)),
                                                3: turn_out(n, t + 2)})
            n = NB - 1
            o = operand(oh, ol)
            job("wo", 0, full, o, {1: turn_fill(TURN["k3"], FILL["qk"] + 2 * NB - 1),
                                   2: then(scores(n, 0), scores(n, 1)),
                                   3: then(turn_probs(n, 0), scores(n, 2)),
                                   4: then(turn_probs(n, 1), scores(n, 3), rows(n, 0), turn_probs(n, 2), rows(n, 1),
                                           turn_probs(n, 3), rows(n, 2), rows(n, 3), turn_out(n, TURN["o3"])),
                                   5: lambda: pe.wait_ge(turn_dve, TURN["o3"] + 1)})
            with pe.Fori(1, NB) as i:
                job("wo", i, full, o, {1: turn_fill(TURN["wo"] - 1 + i, FILL["wo"] - 1 + i)})
            swiglu(1)
            side_operand(1)
            down(1)
            side(1)
            with pe.Fori(0, NB) as i:
                job("ple1", i, full, u)


_INS = ["x", "p", "mix_norm_g", "ffn_norm_g", "ple_norm_g", "ssm_w_in", "ssm_conv_w", "ssm_conv_b", "ssm_dt_bias",
        "ssm_a_log", "ssm_d", "ssm_norm_g", "ssm_w_out", "attn_w_qkv", "attn_w_o", "ffn_w_gate", "ffn_w_up",
        "ffn_w_down", "ple_w_proj", "ple_w_gate", "final_norm_g"]


def kernel(**inputs):
    import numpy as _np
    import concourse.bacc as _bacc
    from concourse import mybir as _mybir
    from concourse.bass_utils import run_bass_kernel_spmd as _run

    nc = _bacc.Bacc("TRN2", target_bir_lowering=False, num_devices=1)
    arrays, args = {}, []
    for name in _INS:
        a = _np.ascontiguousarray(inputs[name])
        arrays[f"in_{name}"] = a
        args.append(nc.dram_tensor(f"in_{name}", a.shape, _mybir.dt.from_np(a.dtype), kind="ExternalInput").ap())
    shape = inputs["x"].shape
    args.append(nc.dram_tensor("out_0", shape, _mybir.dt.float32, kind="ExternalOutput").ap())
    args.append(nc.dram_tensor("cs_scratch", (128, 128), _mybir.dt.float32).ap())
    trunk(nc, *args)
    r = _run(nc, [arrays], core_ids=[0])
    return r.results[0]["out_0"]
```

```python
from contextlib import ExitStack

import concourse.bass as bass
from concourse import mybir

F32 = mybir.dt.float32
F32R = mybir.dt.float32r
BF16 = mybir.dt.bfloat16
ALU = mybir.AluOpType
ACT = mybir.ActivationFunctionType
AX = mybir.AxisListType

P = 128
TOK = 2
RING = 4
CK = 2
BLK = 512
BT = BLK // P
CONV = 4
EPS = 1e-6
NEG = -1.0e30
AHEAD = 5


class Steps:

    def __init__(self):
        self.base, self.k, self.i, self.per = 0, 0, 0, 0

    def next(self):
        self.k += 1
        return self.last()

    def last(self, back=0):
        return self.base + self.k - back + (self.i * self.per if self.per else 0)

    def enter(self, i, per):
        self.base, self.k, self.i, self.per = self.base + self.k, 0, i, per

    def leave(self, times):
        assert self.k == self.per or not self.per, (self.k, self.per)
        self.base, self.k, self.i, self.per = self.base + self.k * times, 0, 0, 0


def trunk(nc, x, p, mix_norm_g, ffn_norm_g, ple_norm_g, ssm_w_in, ssm_conv_w, ssm_conv_b, ssm_dt_bias,
          ssm_a_log, ssm_d, ssm_norm_g, ssm_w_out, attn_w_qkv, attn_w_o, ffn_w_gate, ffn_w_up, ffn_w_down,
          ple_w_proj, ple_w_gate, final_norm_g, out, cs_scratch):
    D = x.shape[2]
    KD = D // P
    NB = D // BLK
    DI = ssm_w_out.shape[1]
    KI = DI // P
    SH = ssm_d.shape[1]
    HD = DI // SH
    G = 8
    HG = SH // G
    CH = ssm_conv_w.shape[2]
    CT = CH // P
    F = ffn_w_gate.shape[2]
    KF = F // P
    FB = F // BLK
    PD = p.shape[3]
    KP = PD // P
    SCALE = float(P) ** -0.5
    assert TOK * P == x.shape[1] and KP == CK and HG * HD == BLK and BT == 4

    full = [CK] * (KD // CK)
    inner = [CK] * (KI // CK)
    hidden = [CK] * 4 + [1] * 4 + [CK] * 16
    assert sum(hidden) == KF and len(hidden) % RING == 0

    order = [("xbc", CH // BLK, len(full)), ("z", G, len(full)), ("wout", NB, len(inner)),
             ("gu0", 2 * FB, len(full)), ("down0", NB, len(hidden)), ("pp0", 2, 2), ("ple0", NB, len(full)),
             ("v", NB, len(full)), ("qk", 2 * NB, len(full)), ("wo", NB, len(full)),
             ("gu1", 2 * FB, len(full)), ("down1", NB, len(hidden)), ("pp1", 2, 2), ("ple1", NB, len(full))]
    CHUNK, JOB, M, c, j = {}, {}, {}, 0, 0
    for name, jobs, m in order:
        CHUNK[name], JOB[name], M[name] = c, j, m
        c, j = c + jobs * m, j + jobs
        assert c % RING == 0
    TURN = {"xbc": NB}
    TURN["z"] = TURN["xbc"] + CH // BLK
    TURN["wout"] = TURN["z"] + G
    TURN["gu0"] = TURN["wout"] + NB
    TURN["down0"] = TURN["gu0"] + FB
    TURN["ple0"] = TURN["down0"] + NB
    TURN["q0"] = TURN["ple0"] + NB
    TURN["qk"] = TURN["q0"] + 1
    TURN["k3"] = TURN["qk"] + 3 * (NB - 1)
    TURN["o3"] = TURN["k3"] + 1
    TURN["wo"] = TURN["o3"] + 1
    TURN["gu1"] = TURN["wo"] + NB
    TURN["down1"] = TURN["gu1"] + FB
    FILL = {"xbc": 0, "z": CH // BLK}
    FILL["wout"] = FILL["z"] + G
    FILL["gu0"] = FILL["wout"] + NB
    FILL["down0"] = FILL["gu0"] + FB
    FILL["ple0"] = FILL["down0"] + NB
    FILL["qk"] = FILL["ple0"] + NB
    FILL["wo"] = FILL["qk"] + 2 * NB
    FILL["gu1"] = FILL["wo"] + NB
    FILL["down1"] = FILL["gu1"] + FB
    FILL["ple1"] = FILL["down1"] + NB
    UPDATE = {"wout": 0, "down0": 1, "ple0": 2, "wo": 3, "down1": 4, "ple1": 5}

    with ExitStack() as ctx:
        KB = 1024
        base = (nc.sbuf_base + 63) // 64 * 64
        ARENA = (nc.sbuf_bytes_remaining - 256) // 64 * 64
        ctx.enter_context(nc.sbuf_tensor("arena", [P, ARENA // 4 + 16], F32))
        at = [0]

        def place(name, shape, off=None, dt=F32):
            size = mybir.dt.size(dt)
            for n in shape[1:]:
                size *= n
            if off is None:
                off = at[0]
                at[0] += (size + 31) // 32 * 32
            assert off + size <= ARENA, (name, off + size)
            return nc.alloc_sbuf_tensor_at(name, shape, dt, offset=base + off)

        def sem(name):
            return ctx.enter_context(nc.semaphore(name))

        h = place("h", [P, TOK, D])
        raw = place("raw", [P, RING, CK, BLK])
        wh = place("wh", [P, RING, CK, BLK], dt=F32R)
        wl = place("wl", [P, RING, CK, BLK], dt=F32R)
        uh = place("uh", [P, KD, TOK * P], dt=F32R)
        ul = place("ul", [P, KD, TOK * P], dt=F32R)
        stage = place("stage", [P, TOK, BLK])
        ident = place("ident", [P, P])
        mask = place("mask", [P, P])
        gains = place("gains", [P, P])
        ssq = place("ssq", [P, TOK, NB])
        pair = place("pair", [P, TOK, 2])
        mean = place("mean", [P, TOK])
        rstd = place("rstd", [P, TOK])
        neghalf = place("neghalf", [P, TOK])
        junk = place("junk", [P, BLK], dt=BF16)
        probe = place("probe", [P, 8])
        conv = place("conv", [P, CONV + 1, CT])
        dt_ = place("dt", [P, TOK, SH])
        cs = place("cs", [P, TOK, SH])
        ecs = place("ecs", [P, SH])
        skip = place("skip", [P, SH])
        gsq = place("gsq", [P, TOK])
        gmean = place("gmean", [P, TOK])
        grstd = place("grstd", [P, TOK])
        big = at[0]
        work = big + 80 * KB
        at[0] = work
        dec = place("dec", [P, TOK, HG, P])
        xdt = place("xdt", [P, TOK, HG, HD])
        xw = place("xw", [P, HG, HD])
        bg = place("bg", [P, TOK * P])
        cg = place("cg", [P, TOK * P])
        btok = place("btok", [P, P])
        xs = place("xs", [P, TOK, HG, HD])
        chan = place("chan", [P, BT, TOK * P], off=work + 8 * KB)
        state = place("state", [P, BLK], off=work + 12 * KB)
        top_of_work = at[0]
        side_at = big + 88 * KB
        xc = place("xc", [P, DI // P, TOK * P], off=big + 32 * KB)
        bc = place("bc", [P, 2 * G, TOK * P], off=big + 64 * KB)
        yt = place("yt", [P, G, 2, BT, TOK * P], off=big, dt=F32R)
        hh = place("hh", [P, KF, TOK * P], off=big, dt=F32R)
        hl = place("hl", [P, KF, TOK * P], off=big + 44 * KB, dt=F32R)
        pp = place("pp", [P, TOK, D], off=big)
        ph = place("ph", [P, KP, TOK * P], off=side_at, dt=F32R)
        pl = place("pl", [P, KP, TOK * P], off=side_at + 2 * KB, dt=F32R)
        prow = place("prow", [P, TOK, PD], off=side_at + 4 * KB)
        vh = place("vh", [P, KD, TOK * P], off=big + 16 * KB, dt=F32R)
        vl = place("vl", [P, KD, TOK * P], off=big + 32 * KB, dt=F32R)
        v = place("v", [P, TOK, D], off=big)
        oh = place("oh", [P, KD, TOK * P], off=big + 48 * KB, dt=F32R)
        ol = place("ol", [P, KD, TOK * P], off=big + 64 * KB, dt=F32R)
        qt = place("qt", [P, BT, TOK * P], off=big + 80 * KB)
        kt = place("kt", [P, BT, TOK * P], off=big + 84 * KB)
        sc = place("sc", [P, 2, 3 * P], off=side_at)
        prt = place("prt", [P, 2, 3, P], off=side_at + 3 * KB)
        orow = place("orow", [P, TOK, BLK], off=side_at + 6 * KB)
        mask3 = place("mask3", [P, 3 * P], off=side_at + 10 * KB)
        top = place("top", [P, BT, 2], off=side_at + 12 * KB)
        ntop = place("ntop", [P, BT, 2], off=side_at + 12 * KB + 64)
        den = place("den", [P, BT, 2], off=side_at + 12 * KB + 128)
        rden = place("rden", [P, BT, 2], off=side_at + 12 * KB + 192)
        fgain = place("fgain", [P, D], off=big + 64 * KB)
        grows = place("grows", [P, P], off=big)
        crows = place("crows", [CT, CONV + 1, P], off=big + 1 * KB)
        draw = place("draw", [P, KD, SH], off=big + 4 * KB)
        dwh = place("dwh", [P, KD, SH], off=big + 8 * KB, dt=F32R)
        dwl = place("dwl", [P, KD, SH], off=big + 12 * KB, dt=F32R)
        upper = place("upper", [P, P], off=big + 16 * KB)
        dtb = place("dtb", [P, SH], off=big + 17 * KB)
        alog = place("alog", [P, SH], off=big + 17 * KB + 256)
        nega = place("nega", [P, SH], off=big + 17 * KB + 512)
        dx = place("dx", [P, TOK * SH], off=big + 18 * KB)
        dabs = place("dabs", [P, TOK * SH], off=big + 18 * KB + 512)
        dexp = place("dexp", [P, TOK * SH], off=big + 19 * KB)
        drel = place("drel", [P, TOK * SH], off=big + 19 * KB + 512)
        dden = place("dden", [P, TOK * SH], off=big + 20 * KB)
        drec = place("drec", [P, TOK * SH], off=big + 20 * KB + 512)
        dy = place("dy", [P, TOK * SH], off=big + 21 * KB)
        dy2 = place("dy2", [P, TOK * SH], off=big + 21 * KB + 512)
        dq = [place(f"dq{n}", [P, TOK * SH], off=big + 22 * KB + 512 * n) for n in range(2)]
        dtt = place("dtt", [SH, TOK * P], off=big + 24 * KB)
        dta = place("dta", [P, TOK, SH], off=big + 23 * KB)
        cst = place("cst", [P, P], off=big + 23 * KB + 512)
        assert top_of_work <= ARENA and side_at + 13 * KB <= ARENA

        def bank(name, shape):
            return ctx.enter_context(nc.psum_tensor(name, shape, F32))

        acc = [bank("acc0", [P, BLK]), bank("acc1", [P, BLK])]
        turned = bank("turned", [P, BT, TOK * P])
        pg = bank("pg", [P, BLK])
        pst = bank("pst", [P, BLK])
        py = bank("py", [P, TOK, BLK])

        load = [sem(f"load{s}") for s in range(RING)]
        hi_done = sem("hi_done")
        lo_done = sem("lo_done")
        mm_done = sem("mm_done")
        acc_done = sem("acc_done")
        acc_free = [sem("acc_free0"), sem("acc_free1")]
        filled = sem("filled")
        turn = sem("turn")
        turn_act = sem("turn_act")
        turn_dve = sem("turn_dve")
        squares = sem("squares")
        h_kept = sem("h_kept")
        rstd_ready = sem("rstd_ready")
        act_step = sem("act_step")
        dve_step = sem("dve_step")
        pool_step = sem("pool_step")
        consts = sem("consts")
        x_in = [sem(f"x_in{b}") for b in range(NB)]
        small_in = sem("small_in")
        dt_in = sem("dt_in")
        bias_in = sem("bias_in")
        gain_turn = sem("gain_turn")
        gain_kept = sem("gain_kept")
        dt_hi = sem("dt_hi")
        dt_lo = sem("dt_lo")
        dt_mm = sem("dt_mm")
        dt_kept = sem("dt_kept")
        dt_x = sem("dt_x")
        dt_act = sem("dt_act")
        dta_done = sem("dta_done")
        cs_mm = sem("cs_mm")
        cs_kept = sem("cs_kept")
        cs_out = sem("cs_out")
        ecs_done = sem("ecs_done")
        conv_bias = sem("conv_bias")
        conv_taps = sem("conv_taps")
        taps_seen = sem("taps_seen")
        conv_out = sem("conv_out")
        group_in = sem("group_in")
        dec_in = sem("dec_in")
        x_turn = sem("x_turn")
        x_kept = sem("x_kept")
        bg_turn = sem("bg_turn")
        b_kept = sem("b_kept")
        xdt_done = sem("xdt_done")
        skip_done = sem("skip_done")
        diff_done = sem("diff_done")
        exp_done = sem("exp_done")
        xw_done = sem("xw_done")
        m_done = sem("m_done")
        st_mm = sem("st_mm")
        st_kept = sem("st_kept")
        ssd_done = sem("ssd_done")
        y_sum = sem("y_sum")
        y_taken = sem("y_taken")
        gated = sem("gated")
        g_squares_step = sem("g_squares_step")
        g_squares = sem("g_squares")
        g_rstd = sem("g_rstd")
        p_in = sem("p_in")
        p_turn = sem("p_turn")
        p_hi = sem("p_hi")
        p_lo = sem("p_lo")
        side_kept = sem("side_kept")
        mask3_done = sem("mask3_done")
        s_mm = sem("s_mm")
        s_top = sem("s_top")
        s_exp = sem("s_exp")
        pr_turn = sem("pr_turn")
        pr_kept = sem("pr_kept")
        o_mm = sem("o_mm")
        o_kept = sem("o_kept")
        fgain_in = sem("fgain_in")
        last_sum = sem("last_sum")
        last_kept = sem("last_kept")
        out_ready = sem("out_ready")
        out_ready_act = sem("out_ready_act")
        out_done = sem("out_done")

        def tiles(w):
            return w.rearrange("(k q) n -> q k n", q=P)

        w_in, w_out = tiles(ssm_w_in[0]), tiles(ssm_w_out[0])
        w_gate = [tiles(ffn_w_gate[l]) for l in range(2)]
        w_up = [tiles(ffn_w_up[l]) for l in range(2)]
        w_down = [tiles(ffn_w_down[l]) for l in range(2)]
        w_qkv, w_o = tiles(attn_w_qkv[0]), tiles(attn_w_o[0])
        w_pg = [tiles(ple_w_gate[l]) for l in range(2)]
        w_pp = [tiles(ple_w_proj[l]) for l in range(2)]
        x_rows = x[0].rearrange("(t q) n -> q t n", q=P)
        out_rows = out[0].rearrange("(t q) n -> q t n", q=P)

        def half(b):
            return turned[:, :, :] if b % 2 == 0 else py[:, :, :].rearrange("q t (k n) -> q (t k) n", k=2)

        def apart(eng):
            eng.wait_ge(consts, 1)

        def bank_ready(eng, t, phase, i):
            if t == 0:
                eng.wait_ge(acc_done, JOB[phase] + i + 1)
            else:
                eng.wait_ge(mm_done, CHUNK[phase] + (i + 1) * M[phase])

        def block_of(tensor, b):
            return tensor[:, :, bass.ds(b * BLK, BLK)]

        GAIN = {"mix0": 0, "mix1": KD, "ffn0": 2 * KD, "ffn1": 3 * KD, "ple0": 4 * KD, "ple1": 5 * KD, "ssm": 6 * KD}

        block = ctx.enter_context(nc.Block())

        @block.sync
        def _(sp):
            def chunk(c, n, tiles, src):
                s = n % RING
                if not (isinstance(c, int) and c < RING):
                    sp.wait_ge(lo_done, c - RING + 1)
                sp.dma_start(raw[:, s, 0:tiles, :], src).then_inc(load[s], 16)

            def job(w, col, c, sizes, first=0):
                k = 0
                for n, size in enumerate(sizes):
                    if n >= first:
                        chunk(c + n, n, size, w[:, k:k + size, bass.ds(col, BLK)])
                    k += size

            def first_chunk(n):
                chunk(n, n, CK, w_in[:, CK * n:CK * (n + 1), 2 * DI:2 * DI + BLK])

            for b in range(NB):
                sp.dma_start(block_of(h, b), block_of(x_rows, b)).then_inc(x_in[b], 16)
                if b == 1:
                    for n in range(3):
                        first_chunk(n)
                if b == 2:
                    first_chunk(3)
                if b == 0:
                    rows = 0
                    for g in (mix_norm_g, ffn_norm_g, ple_norm_g, ssm_norm_g):
                        n = 2 * KD
                        sp.dma_start(grows[rows:rows + n, :], g.rearrange("l (k q) -> (l k) q", q=P)
                                     ).then_inc(small_in, 16)
                        rows += n
                    sp.dma_start(crows[:, 0:CONV, :], ssm_conv_w[0].rearrange("j (k q) -> k j q", q=P)
                                 ).then_inc(small_in, 16)
                    sp.dma_start(crows[:, CONV, :], ssm_conv_b[0].rearrange("(k q) -> k q", q=P)
                                 ).then_inc(small_in, 16)
            c = CHUNK["xbc"]
            m = len(full)
            job(w_in, 2 * DI, c, full, first=RING)
            sp.dma_start(draw[:, :, :], w_in[:, :, 2 * DI + 2 * G * P:2 * DI + 2 * G * P + SH]).then_inc(dt_in, 16)
            for dst, src in ((dtb, ssm_dt_bias), (alog, ssm_a_log), (skip, ssm_d)):
                sp.dma_start(dst[:, :], src[0:1, :].broadcast_to([P, SH])).then_inc(bias_in, 16)
            with sp.Fori(1, 4) as i:
                job(w_in, 2 * DI + i * BLK, c + i * m, full)
            c += 4 * m
            with sp.Fori(0, G) as i:
                job(w_in, DI + i * BLK, c + i * m, full)
            with sp.Fori(0, G) as i:
                job(w_in, i * BLK, CHUNK["z"] + i * m, full)
            with sp.Fori(0, NB) as i:
                job(w_out, i * BLK, CHUNK["wout"] + i * len(inner), inner)
            for l in range(2):
                if l == 1:
                    with sp.Fori(0, NB) as i:
                        job(w_qkv, 2 * D + i * BLK, CHUNK["v"] + i * m, full)
                    with sp.Fori(0, NB) as i:
                        job(w_qkv, i * BLK, CHUNK["qk"] + i * 2 * m, full)
                        job(w_qkv, D + i * BLK, CHUNK["qk"] + i * 2 * m + m, full)
                    with sp.Fori(0, NB) as i:
                        job(w_o, i * BLK, CHUNK["wo"] + i * m, full)
                with sp.Fori(0, FB) as i:
                    job(w_gate[l], i * BLK, CHUNK[f"gu{l}"] + i * 2 * m, full)
                    job(w_up[l], i * BLK, CHUNK[f"gu{l}"] + i * 2 * m + m, full)
                with sp.Fori(0, NB) as i:
                    job(w_down[l], i * BLK, CHUNK[f"down{l}"] + i * len(hidden), hidden)
                for b in range(NB):
                    chunk(CHUNK[f"pp{l}"] + b, b, CK, w_pp[l][:, :, b * BLK:(b + 1) * BLK])
                with sp.Fori(0, NB) as i:
                    job(w_pg[l], i * BLK, CHUNK[f"ple{l}"] + i * m, full)
            for b in range(NB):
                sp.wait_ge(out_ready, b + 1)
                sp.wait_ge(out_ready_act, b + 1)
                sp.dma_start(block_of(out_rows, b), block_of(h, b)).then_inc(out_done, 16)
            sp.wait_ge(out_done, NB * 16)

        @block.gpsimd
        def _(pool):
            st = Steps()

            def done():
                pool.wait_ge(pool_step, st.last())

            def step(ins):
                ins.then_inc(pool_step, 1)
                st.next()

            step(pool.memset(ident[:, :], 0.0))
            step(pool.memset(mask[:, :], 0.0))
            step(pool.memset(upper[:, :], 1.0))
            step(pool.memset(neghalf[:, :], -0.5))
            done()
            step(pool.affine_select(out=ident[:, :], in_=ident[:, :], compare_op=ALU.not_equal, fill=1.0,
                                    base=0, pattern=[[-1, P]], channel_multiplier=1))
            step(pool.affine_select(out=mask[:, :], in_=mask[:, :], compare_op=ALU.is_ge, fill=NEG,
                                    base=0, pattern=[[1, P]], channel_multiplier=-1))
            step(pool.affine_select(out=upper[:, :], in_=upper[:, :], compare_op=ALU.is_ge, fill=0.0,
                                    base=0, pattern=[[1, P]], channel_multiplier=-1))
            done()
            pool.nop().then_inc(consts, 1)

            def finish_scales():
                step(pool.tensor_scalar(mean[:, :], mean[:, :], 1.0 / D, EPS, ALU.mult, ALU.add))
                done()
                pool.tensor_tensor(rstd[:, :], mean[:, :], neghalf[:, :], ALU.pow).then_inc(rstd_ready, 1)

            def row_scales(sums):
                pool.wait_ge(squares, sums)
                step(pool.tensor_tensor(pair[:, :, :], ssq[:, :, 0:2], ssq[:, :, 2:4], ALU.add))
                done()
                step(pool.tensor_tensor(mean[:, :], pair[:, :, 0], pair[:, :, 1], ALU.add))
                done()
                finish_scales()

            row_scales(NB)

            pool.wait_ge(cs_kept, 2)
            pool.dma_start(cs_scratch, cst[:, :]).then_inc(cs_out, 16)
            pool.wait_ge(cs_out, 16)

            def load_rows(g):
                pool.dma_start(dec[:, :, :, :].rearrange("q c h l -> q c (h l)"),
                               cs_scratch.rearrange("(c r) l -> c (r l)", c=TOK)[:, bass.ds(g * HG * P, HG * P)]
                               .rearrange("(o c) n -> o c n", o=1).broadcast_to([P, TOK, HG * P])
                               ).then_inc(dec_in, 16)

            load_rows(0)
            pool.wait_ge(conv_out, 5)
            pool.tensor_copy(chan[:, :, :], xc[:, 0:BT, :]).then_inc(group_in, 1)
            pool.tensor_copy(bg[:, :], bc[:, 0, :]).then_inc(group_in, 1)
            pool.tensor_copy(cg[:, :], bc[:, G, :]).then_inc(group_in, 1)

            def group(g, last=False):
                pool.wait_ge(x_kept, g + 1)
                pool.tensor_tensor(xdt[:, :, :, :], xs[:, :, :, :],
                                   dt_[:, :, bass.ds(g * HG, HG)].rearrange("q c (h o) -> q c h o", o=1)
                                   .broadcast_to([P, TOK, HG, HD]), ALU.mult).then_inc(xdt_done, 1)
                pool.wait_ge(xdt_done, g + 1)
                pool.tensor_tensor(xs[:, :, :, :], xs[:, :, :, :],
                                   skip[:, bass.ds(g * HG, HG)].rearrange("q (c h o) -> q c h o", o=1, c=1)
                                   .broadcast_to([P, TOK, HG, HD]), ALU.mult).then_inc(skip_done, 1)
                if not last:
                    pool.wait_ge(ssd_done, g + 1)
                    load_rows(g + 1)
                pool.wait_ge(g_squares, g + 1)
                step(pool.nop())
                step(pool.tensor_scalar(gmean[:, :], gsq[:, :], 1.0 / BLK, EPS, ALU.mult, ALU.add))
                done()
                pool.tensor_tensor(grstd[:, :], gmean[:, :], neghalf[:, :], ALU.pow).then_inc(g_rstd, 1)

            with pool.Fori(0, G - 1) as g:
                st.enter(g, 2)
                group(g)
            st.leave(G - 1)
            group(G - 1, last=True)

            def keep_h(phase):
                u = UPDATE[phase]
                with pool.Fori(0, NB) as i:
                    pool.wait_ge(filled, FILL[phase] + i + 1)
                    pool.tensor_copy(block_of(h, i), stage[:, :, :]).then_inc(h_kept, 1)
                row_scales(NB * (u + 2))

            keep_h("wout")
            pool.dma_start(prow[:, :, :], p[0, 0].rearrange("(t q) n -> q t n", q=P)).then_inc(p_in, 16)
            keep_h("down0")
            keep_h("ple0")
            pool.wait_ge(mm_done, CHUNK["ple0"])
            pool.wait_ge(turn, TURN["ple0"])
            step(pool.memset(mask3[:, :], 0.0))
            done()
            for n in (0, 2):
                step(pool.affine_select(out=mask3[:, n * P:(n + 1) * P], in_=mask3[:, n * P:(n + 1) * P],
                                        compare_op=ALU.is_ge, fill=NEG, base=0, pattern=[[-1, P]],
                                        channel_multiplier=1))
            done()
            pool.nop().then_inc(mask3_done, 1)
            keep_h("wo")
            pool.dma_start(prow[:, :, :], p[1, 0].rearrange("(t q) n -> q t n", q=P)).then_inc(p_in, 16)
            keep_h("down1")
            pool.dma_start(fgain[:, :], final_norm_g.rearrange("(o n) -> o n", o=1).broadcast_to([P, D])
                           ).then_inc(fgain_in, 16)
            pool.wait_ge(fgain_in, 16)
            with pool.Fori(0, NB - 1) as i:
                pool.wait_ge(filled, FILL["ple1"] + i + 1)
                pool.tensor_tensor(block_of(h, i), stage[:, :, :],
                                   fgain[:, bass.ds(i * BLK, BLK)].rearrange("q (o n) -> q o n", o=1)
                                   .broadcast_to([P, TOK, BLK]), ALU.mult).then_inc(h_kept, 1)
            pool.wait_ge(squares, NB * 7 - 1)
            step(pool.tensor_tensor(pair[:, :, 0:1], ssq[:, :, 0:1], ssq[:, :, 1:2], ALU.add))
            done()
            step(pool.tensor_tensor(pair[:, :, 1:2], pair[:, :, 0:1], ssq[:, :, 2:3], ALU.add))
            done()
            pool.wait_ge(squares, NB * 7)
            step(pool.tensor_tensor(mean[:, :], pair[:, :, 1], ssq[:, :, 3], ALU.add))
            done()
            finish_scales()

        @block.scalar
        def _(act):
            st = Steps()

            def hi(c, n, tiles=CK, uses=None):
                s = n % RING
                act.wait_ge(load[s], uses)
                if not (isinstance(c, int) and c < RING):
                    act.wait_ge(mm_done, c - RING + 1)
                nc.scalar.activation(wh[:, s, 0:tiles, :], raw[:, s, 0:tiles, :], ACT.Copy).then_inc(hi_done, 1)

            def hi_of(phase, i, m, first, last, sizes=None):
                for n in range(first, last):
                    c = CHUNK[phase] + i * m + n
                    uses = 16 * ((CHUNK[phase] + n) // RING + 1) + i * (16 * m // RING)
                    hi(c, n, sizes[n] if sizes and n < m else CK, uses)

            def turned_hi(t, dst, gain=None):
                act.wait_ge(turn, t + 1)
                apart(act)
                if gain is None:
                    nc.scalar.activation(dst, turned[:, :, :], ACT.Copy).then_inc(turn_act, 1)
                    return
                for k in range(BT):
                    ins = nc.scalar.activation(dst[:, k, :], turned[:, k, :], ACT.Copy, scale=gain(k))
                ins.then_inc(turn_act, 1)

            def gain_of(name, first):
                return lambda k: gains[:, bass.ds(GAIN[name] + first + k, 1)]

            def use_table(n, func):
                nc.scalar.activation(probe[:, n:n + 1], ident[:, 0:1], func)

            act.wait_ge(consts, 1)
            use_table(0, ACT.Silu)

            def turned_x(b):
                if b == 0:
                    act.wait_ge(gain_kept, 2)
                act.wait_ge(turn, b + 1)
                for k in range(BT):
                    ins = nc.scalar.activation(uh[:, b * BT + k, :], half(b)[:, k, :], ACT.Copy,
                                               scale=gain_of("mix0", b * BT)(k))
                ins.then_inc(turn_act, 1)

            def first_hi(n):
                hi(n, n, CK, 16 * (n // RING + 1))

            def squares_of(b):
                for t in range(TOK):
                    if t or b:
                        act.wait_ge(act_step, st.last())
                    nc.scalar.activation(junk[:, :], h[:, t, b * BLK:(b + 1) * BLK], ACT.Square,
                                         accum_out=ssq[:, t, b:b + 1]).then_inc(act_step, 1)
                    st.next()
                act.wait_ge(act_step, st.last())
                act.nop().then_inc(squares, 1)

            turned_x(0)
            first_hi(0)
            turned_x(1)
            first_hi(1)
            first_hi(2)
            turned_x(2)
            first_hi(3)
            first_hi(4)
            turned_x(3)
            squares_of(0)
            first_hi(5)
            squares_of(1)
            squares_of(2)
            first_hi(6)
            squares_of(3)
            first_hi(7)
            act.wait_ge(dt_in, 16)
            nc.scalar.activation(dwh[:, :, :], draw[:, :, :], ACT.Copy).then_inc(dt_hi, 1)

            def softplus_parts():
                act.wait_ge(bias_in, 48)
                nc.scalar.activation(nega[:, :], alog[:, :], ACT.Exp).then_inc(dt_act, 1)
                act.wait_ge(dt_x, 1)
                nc.scalar.activation(dabs[:, :], dx[:, :], ACT.Abs).then_inc(dt_act, 1)
                act.wait_ge(dt_act, 2)
                nc.scalar.activation(dexp[:, :], dabs[:, :], ACT.Exp, scale=-1.0).then_inc(dt_act, 1)
                nc.scalar.activation(drel[:, :], dx[:, :], ACT.Relu).then_inc(dt_act, 1)

            m = len(full)

            def conv_bias_part(out_tiles, tile0, t):
                act.wait_ge(turn, t + 1)
                apart(act)
                for k in range(BT):
                    w = tile0 + k + (DI // P if out_tiles is bc else 0)
                    nc.scalar.activation(out_tiles[:, bass.ds(tile0 + k, 1), :], turned[:, k, :], ACT.Identity,
                                         bias=conv[:, CONV, bass.ds(w, 1)], scale=conv[:, CONV - 1, bass.ds(w, 1)]
                                         ).then_inc(conv_bias, 1)
                act.wait_ge(conv_bias, BT * (t - TURN["xbc"] + 1))
                act.nop().then_inc(turn_act, 1)

            def conv_silu(out_tiles, tile0, t):
                act.wait_ge(conv_taps, t - TURN["xbc"] + 1)
                act.nop().then_inc(taps_seen, 1)
                part = out_tiles[:, bass.ds(tile0, BT), :]
                nc.scalar.activation(part, part, ACT.Silu).then_inc(conv_out, 1)

            def conv_job(i, out_tiles, tile0):
                conv_bias_part(out_tiles, tile0, TURN["xbc"] + i - 1)
                hi_of("xbc", i, m, AHEAD, m)
                conv_silu(out_tiles, tile0, TURN["xbc"] + i - 1)
                hi_of("xbc", i, m, m, m + AHEAD)

            hi_of("xbc", 0, m, m, m + 4)
            softplus_parts()
            hi_of("xbc", 0, m, m + 4, m + AHEAD)
            use_table(6, ACT.Silu)
            conv_job(1, bc, 0)
            with act.Fori(2, 5) as i:
                conv_job(i, bc, i * BT - BT)
            with act.Fori(5, CH // BLK) as i:
                conv_job(i, xc, i * BT - 5 * BT)

            act.wait_ge(cs_kept, 1)
            nc.scalar.activation(ecs[:, :], cs[:, 1, :], ACT.Exp).then_inc(ecs_done, 1)

            def turned_y(g):
                turned_hi(TURN["z"] + g, yt[:, bass.ds(g, 1), 0, :, :].rearrange("q o k n -> q (o k) n"),
                          lambda k: gains[:, bass.ds(GAIN["ssm"] + g * BT + k, 1)])

            def z_job(g, first=False):
                act.wait_ge(x_turn, g + 1)
                if not first:
                    act.wait_ge(gated, g)
                nc.scalar.activation(xs[:, :, :, :].rearrange("q c h d -> q c (h d)"), py[:, :, :],
                                     ACT.Copy).then_inc(x_kept, 1)
                act.wait_ge(bg_turn, g + 1)
                nc.scalar.activation(btok[:, :], pg[:, TOK * P:(TOK + 1) * P], ACT.Copy).then_inc(b_kept, 1)
                if not first:
                    hi_of("z", g, m, AHEAD - 1, AHEAD)
                act.wait_ge(diff_done, g + 1)
                nc.scalar.activation(dec[:, :, :, :], dec[:, :, :, :], ACT.Exp).then_inc(exp_done, 1)
                hi_of("z", g, m, AHEAD, AHEAD + 1)
                if first:
                    conv_bias_part(xc, (G - 1) * BT, TURN["z"] - 1)
                else:
                    turned_y(g - 1)
                hi_of("z", g, m, AHEAD + 1, m)
                act.wait_ge(st_mm, g + 1)
                nc.scalar.activation(state[:, :], pst[:, :], ACT.Copy).then_inc(st_kept, 1)
                if first:
                    conv_silu(xc, (G - 1) * BT, TURN["z"] - 1)
                else:
                    use_table(5, ACT.Silu)
                hi_of("z", g, m, m, m + 3)
                act.wait_ge(turn, TURN["z"] + g)
                act.wait_ge(rstd_ready, 1)
                for t in range(TOK):
                    bank_ready(act, t, "z", g)
                    nc.scalar.activation(stage[:, t, :], acc[t][:, :], ACT.Silu, scale=rstd[:, t:t + 1]
                                         ).then_inc(acc_free[t], 1)
                act.wait_ge(gated, g + 1)
                for t in range(TOK):
                    nc.scalar.activation(junk[:, :], stage[:, t, :], ACT.Square, accum_out=gsq[:, t:t + 1]
                                         ).then_inc(g_squares_step, 1)
                    act.wait_ge(g_squares_step, 2 * g + t + 1)
                act.nop().then_inc(g_squares, 1)
                hi_of("z", g, m, m + 3, m + 4)

            z_job(0, first=True)
            with act.Fori(1, G) as g:
                z_job(g)
            hi_of("wout", 0, len(inner), AHEAD - 1, AHEAD)
            turned_y(G - 1)

            def sum_squares(phase, i, last=False):
                if not last:
                    act.wait_ge(filled, FILL[phase] + i + 1)
                for t in range(TOK):
                    if last:
                        act.wait_ge(last_sum, t + 1)
                    else:
                        apart(act)
                    nc.scalar.activation(junk[:, :], stage[:, t, :], ACT.Square,
                                         accum_out=ssq[:, t, bass.ds(i, 1)]).then_inc(act_step, 1)
                    st.next()
                    act.wait_ge(act_step, st.last())
                act.nop().then_inc(squares, 1)

            def update(phase, sizes, dst, gain):
                m = len(sizes)
                with act.Fori(0, NB) as i:
                    st.enter(i, 2)
                    hi_of(phase, i, m, AHEAD, m + 3, sizes)
                    sum_squares(phase, i)
                    hi_of(phase, i, m, m + 3, m + AHEAD)
                    turned_hi(TURN[phase] + i, dst[:, bass.ds(i * BT, BT), :],
                              lambda k: gains[:, bass.ds(GAIN[gain] + i * BT + k, 1)])
                st.leave(NB)

            def swiglu(l):
                m, name = len(full), f"gu{l}"
                with act.Fori(0, FB) as i:
                    hi_of(name, 2 * i, m, AHEAD, m + 3)
                    act.wait_ge(turn, TURN[name] + i)
                    act.wait_ge(h_kept, NB * (UPDATE["wo" if l else "wout"] + 1))
                    act.wait_ge(rstd_ready, 5 if l else 2)
                    for t in range(TOK):
                        bank_ready(act, t, name, 2 * i)
                        nc.scalar.activation(stage[:, t, :], acc[t][:, :], ACT.Silu, scale=rstd[:, t:t + 1]
                                             ).then_inc(acc_free[t], 1)
                    hi_of(name, 2 * i, m, m + 3, 2 * m + 3)
                    hi_of(name, 2 * i, m, 2 * m + 3, 2 * m + AHEAD)
                    turned_hi(TURN[name] + i, hh[:, bass.ds(i * BT, BT), :])

            def side_operand(l):
                act.wait_ge(p_turn, l + 1)
                nc.scalar.activation(ph[:, :, :].rearrange("q k n -> q (k n)"), pst[:, :], ACT.Copy).then_inc(p_hi, 1)

            def side(l):
                c = CHUNK[f"pp{l}"]
                for b, parts in ((1, (py[:, 0, :], py[:, 1, :])), (2, (pg[:, :], pst[:, :]))):
                    hi(c + AHEAD + b - 1, b, CK, 16 * ((c + AHEAD + b - 1) // RING + 1))
                    act.wait_ge(mm_done, c + b + 1)
                    for t in range(TOK):
                        nc.scalar.activation(pp[:, t, b * BLK:(b + 1) * BLK], parts[t], ACT.Copy
                                             ).then_inc(side_kept, 1)
                for n in range(AHEAD + 2, AHEAD + 4):
                    hi(c + n, n, CK, 16 * ((c + n) // RING + 1))

            def gate_update(l, i, dst=None, gain=None, last=False):
                m, name = len(full), f"ple{l}"
                if last:
                    hi_of(name, i, m, AHEAD, m)
                else:
                    hi_of(name, i, m, AHEAD, m + 3)
                act.wait_ge(turn, TURN["ple0"] + i if l == 0 else TURN["down1"] + NB)
                act.wait_ge(h_kept, NB * UPDATE[name] + i)
                act.wait_ge(rstd_ready, 3 + 3 * l)
                for t in range(TOK):
                    bank_ready(act, t, name, i)
                    nc.scalar.activation(stage[:, t, :], acc[t][:, :], ACT.Sigmoid, scale=rstd[:, t:t + 1]
                                         ).then_inc(acc_free[t], 1)
                sum_squares(name, i, last)
                if not last:
                    hi_of(name, i, m, m + 3, m + AHEAD)
                if dst is not None:
                    turned_hi(TURN[name] + i, dst[:, bass.ds(i * BT, BT), :],
                              lambda k: gains[:, bass.ds(GAIN[gain] + i * BT + k, 1)])

            def exps(n, hd):
                act.wait_ge(s_top, n * BT + hd + 1)
                for q, (lo, up) in enumerate(((0, P), (P, 3 * P))):
                    nc.scalar.activation(sc[:, hd % 2, lo:up], sc[:, hd % 2, lo:up], ACT.Exp,
                                         bias=ntop[:, hd, q:q + 1], scale=SCALE,
                                         accum_out=den[:, hd, q:q + 1]).then_inc(s_exp, 1)

            def evac_scaled(phase, i, dst, fill=True):
                for t in range(TOK):
                    bank_ready(act, t, phase, i)
                    apart(act)
                    nc.scalar.activation(dst[:, t, :], acc[t][:, :], ACT.Copy, scale=rstd[:, t:t + 1]
                                         ).then_inc(acc_free[t], 1)
                if fill:
                    act.wait_ge(acc_free[0], JOB[phase] + i + 2)
                    act.wait_ge(acc_free[1], JOB[phase] + i + 2)
                    act.nop().then_inc(filled, 1)

            def half_turned(t, dst):
                act.wait_ge(turn, t + 1)
                nc.scalar.activation(dst[:, 0:2, :], turned[:, 0:2, :], ACT.Copy).then_inc(turn_act, 1)

            update("wout", inner, uh, "ffn0")
            swiglu(0)
            side_operand(0)
            use_table(1, ACT.Sigmoid)
            update("down0", hidden, uh, "ple0")
            side(0)
            with act.Fori(0, NB) as i:
                st.enter(i, 2)
                gate_update(0, i, vh, "mix1")
            st.leave(NB)
            use_table(2, ACT.Exp)
            with act.Fori(0, NB) as i:
                hi_of("v", i, m, AHEAD, m + 3)
                act.wait_ge(rstd_ready, 4)
                evac_scaled("v", i, block_of(v, i), fill=False)
                hi_of("v", i, m, m + 3, m + AHEAD)

            def qk_pair(j, attend):
                hi_of("qk", 2 * j, m, AHEAD, m)
                if attend:
                    exps(j - 1, 0)
                    exps(j - 1, 1)
                hi_of("qk", 2 * j, m, m, m + 2)
                if attend:
                    exps(j - 1, 2)
                hi_of("qk", 2 * j, m, m + 2, m + 3)
                if attend:
                    act.wait_ge(turn, TURN["qk"] + 3 * (j - 1) + 1)
                else:
                    act.wait_ge(turn, TURN["q0"])
                    act.wait_ge(h_kept, NB * (UPDATE["ple0"] + 1))
                evac_scaled("qk", 2 * j, stage)
                if attend:
                    exps(j - 1, 3)
                hi_of("qk", 2 * j, m, m + 3, m + AHEAD)
                tq = TURN["qk"] + 3 * (j - 1) + 1 if attend else TURN["q0"]
                if attend:
                    act.wait_ge(s_mm, BT * j)
                half_turned(tq, qt)
                hi_of("qk", 2 * j, m, m + AHEAD, 2 * m)
                if attend:
                    to = TURN["qk"] + 3 * (j - 1) + 2
                    turned_hi(to, oh[:, bass.ds((j - 1) * BT, BT), :])
                hi_of("qk", 2 * j, m, 2 * m, 2 * m + 3)
                act.wait_ge(turn, tq + 1)
                evac_scaled("qk", 2 * j + 1, stage)
                hi_of("qk", 2 * j, m, 2 * m + 3, 2 * m + AHEAD)
                tk = TURN["qk"] + 3 * j if attend else TURN["qk"]
                half_turned(tk, kt)

            qk_pair(0, False)
            with act.Fori(1, NB) as j:
                qk_pair(j, True)
            hi_of("wo", 0, m, AHEAD, AHEAD + 1)
            exps(NB - 1, 0)
            exps(NB - 1, 1)
            hi_of("wo", 0, m, AHEAD + 1, AHEAD + 2)
            exps(NB - 1, 2)
            exps(NB - 1, 3)
            hi_of("wo", 0, m, AHEAD + 2, m)
            turned_hi(TURN["o3"], oh[:, (NB - 1) * BT:NB * BT, :])

            def wo_rest(i):
                sum_squares("wo", i)
                hi_of("wo", i, m, m + 3, m + AHEAD)
                turned_hi(TURN["wo"] + i, uh[:, bass.ds(i * BT, BT), :],
                          lambda k: gains[:, bass.ds(GAIN["ffn1"] + i * BT + k, 1)])

            hi_of("wo", 0, m, m, m + 3)
            wo_rest(0)
            use_table(3, ACT.Silu)
            with act.Fori(1, NB) as i:
                st.base -= 2
                st.enter(i, 2)
                hi_of("wo", i, m, AHEAD, m + 3)
                wo_rest(i)
            st.leave(NB)
            swiglu(1)
            side_operand(1)
            use_table(4, ACT.Sigmoid)
            update("down1", hidden, uh, "ple1")
            side(1)
            with act.Fori(0, NB - 1) as i:
                st.enter(i, 2)
                gate_update(1, i)
            st.leave(NB - 1)
            gate_update(1, NB - 1, last=True)
            act.wait_ge(rstd_ready, 7)
            act.wait_ge(h_kept, NB * 6 - 1)
            for b in range(NB):
                if b == NB - 1:
                    act.wait_ge(last_kept, TOK)
                o = h[:, 1, b * BLK:(b + 1) * BLK]
                nc.scalar.activation(o, o, ACT.Copy, scale=rstd[:, 1:2]).then_inc(out_ready_act, 1)

        @block.vector
        def _(dve):
            st = Steps()

            def lo(c, n, tiles=CK):
                s = n % RING
                dve.wait_ge(hi_done, c + 1)
                nc.vector.tensor_tensor(wl[:, s, 0:tiles, :], raw[:, s, 0:tiles, :],
                                        wh[:, s, 0:tiles, :].bitcast(F32), ALU.subtract).then_inc(lo_done, 1)

            def lo_of(phase, i, m, first, last, sizes=None):
                for n in range(first, last):
                    lo(CHUNK[phase] + i * m + n, n, sizes[n] if sizes and n < m else CK)

            def turned_lo(t, dst, high, gain=None, src=turned):
                dve.wait_ge(turn_act, t + 1)
                if gain is None:
                    nc.vector.tensor_tensor(dst, turned[:, :, :], high.bitcast(F32), ALU.subtract
                                            ).then_inc(turn_dve, 1)
                    return
                for k in range(BT):
                    ins = nc.vector.scalar_tensor_tensor(out=dst[:, k, :], in0=src[:, k, :], scalar=gain(k),
                                                         in1=high[:, k, :].bitcast(F32), op0=ALU.mult,
                                                         op1=ALU.subtract)
                ins.then_inc(turn_dve, 1)

            def step(ins):
                ins.then_inc(dve_step, 1)
                st.next()

            def done(back=0):
                dve.wait_ge(dve_step, st.last(back))

            dve.wait_ge(gain_turn, 1)
            nc.vector.tensor_copy(gains[:, :], acc[0][:, 0:P]).then_inc(gain_kept, 1)
            dve.wait_ge(gain_turn, 2)
            nc.vector.tensor_copy(conv[:, :, :].rearrange("q j k -> q (j k)"), acc[1][:, 0:(CONV + 1) * CT]
                                  ).then_inc(gain_kept, 1)
            dve.wait_ge(gain_kept, 2)
            dve.nop().then_inc(acc_free[0], 1)
            dve.nop().then_inc(acc_free[1], 1)

            def turned_x(b):
                turned_lo(b, ul[:, b * BT:(b + 1) * BT, :], uh[:, b * BT:(b + 1) * BT, :],
                          lambda k: gains[:, GAIN["mix0"] + b * BT + k:GAIN["mix0"] + b * BT + k + 1], half(b))

            turned_x(0)
            lo(0, 0)
            turned_x(1)
            lo(1, 1)
            lo(2, 2)
            turned_x(2)
            lo(3, 3)
            lo(4, 4)
            turned_x(3)
            for n in range(5, 8):
                lo(n, n)
            dve.wait_ge(dt_hi, 1)
            nc.vector.tensor_tensor(dwl[:, :, :], draw[:, :, :], dwh[:, :, :].bitcast(F32), ALU.subtract
                                    ).then_inc(dt_lo, 1)
            m = len(full)

            def keep_dt():
                dve.wait_ge(dt_mm, 1)
                step(nc.vector.tensor_copy(dtt[:, :], pg[0:SH, 0:TOK * P]))
                done()
                dve.nop().then_inc(dt_kept, 1)
                dve.nop().then_inc(m_done, 1)

            def dt_rows():
                dve.wait_ge(dt_mm, 2)
                dve.wait_ge(bias_in, 48)
                for t in range(TOK):
                    step(nc.vector.scalar_tensor_tensor(out=dx[:, t * SH:(t + 1) * SH], in0=py[:, 0, t * SH:(t + 1) * SH],
                                                        scalar=rstd[:, t:t + 1], in1=dtb[:, :], op0=ALU.mult, op1=ALU.add))
                done()
                dve.nop().then_inc(dt_x, 1)
                dve.nop().then_inc(y_taken, 1)

            def softplus():
                dve.wait_ge(dt_act, 4)
                step(nc.vector.tensor_scalar(dden[:, :], dexp[:, :], 2.0, None, ALU.add))
                done()
                step(nc.vector.reciprocal(drec[:, :], dden[:, :]))
                done()
                step(nc.vector.tensor_tensor(dy[:, :], dexp[:, :], drec[:, :], ALU.mult))
                done()
                step(nc.vector.tensor_tensor(dy2[:, :], dy[:, :], dy[:, :], ALU.mult))
                done()
                step(nc.vector.tensor_scalar(dq[0][:, :], dy2[:, :], 1.0 / 17, None, ALU.mult))
                done()
                for n, term in enumerate((15, 13, 11, 9, 7, 5, 3)):
                    step(nc.vector.scalar_tensor_tensor(out=dq[1 - n % 2][:, :], in0=dq[n % 2][:, :], scalar=1.0 / term,
                                                        in1=dy2[:, :], op0=ALU.add, op1=ALU.mult))
                    done()
                step(nc.vector.scalar_tensor_tensor(out=dq[0][:, :], in0=dq[1][:, :], scalar=1.0, in1=dy[:, :],
                                                    op0=ALU.add, op1=ALU.mult))
                done()
                step(nc.vector.scalar_tensor_tensor(out=dt_[:, :, :].rearrange("q t h -> q (t h)"), in0=dq[0][:, :],
                                                    scalar=2.0, in1=drel[:, :], op0=ALU.mult, op1=ALU.add))
                done()
                for t in range(TOK):
                    step(nc.vector.scalar_tensor_tensor(out=dta[:, t, :], in0=dt_[:, t, :], scalar=-1.0, in1=nega[:, :],
                                                        op0=ALU.mult, op1=ALU.mult))
                done()
                dve.nop().then_inc(dta_done, 1)

            def keep_sums():
                dve.wait_ge(cs_mm, 1)
                step(nc.vector.tensor_copy(cs[:, :, :].rearrange("q t h -> q (t h)"), py[:, 1, 0:TOK * SH]))
                done()
                dve.nop().then_inc(cs_kept, 1)

            def keep_turned_sums():
                dve.wait_ge(cs_mm, 2)
                step(nc.vector.tensor_copy(cst[:, :], py[:, 1, TOK * SH:TOK * SH + P]))
                done()
                dve.nop().then_inc(cs_kept, 1)

            def taps(out_tiles, tile0, t, rows):
                n = TOK * P
                for tap in rows:
                    back = CONV - 1 - tap
                    for k in range(BT):
                        if back == 1:
                            dve.wait_ge(conv_bias, BT * (t - TURN["xbc"] + 1))
                        else:
                            done(BT - 1)
                        o = out_tiles[:, bass.ds(tile0 + k, 1), back:n]
                        w = tile0 + k + (DI // P if out_tiles is bc else 0)
                        step(nc.vector.scalar_tensor_tensor(out=o, in0=turned[:, k:k + 1, 0:n - back],
                                                            scalar=conv[:, tap, bass.ds(w, 1)], in1=o,
                                                            op0=ALU.mult, op1=ALU.add))

            def conv_part(phase, i, out_tiles, tile0, t, start=AHEAD):
                taps(out_tiles, tile0, t, (2, 1))
                lo_of(phase, i, m, start, start + 1)
                taps(out_tiles, tile0, t, (0,))
                done()
                dve.nop().then_inc(turn_dve, 1)
                dve.nop().then_inc(conv_taps, 1)
                lo_of(phase, i, m, start + 1, AHEAD + 2)

            def to_stage(i):
                dve.wait_ge(turn, TURN["xbc"] + i)
                for a in range(TOK):
                    bank_ready(dve, a, "xbc", i)
                    nc.vector.tensor_scalar(stage[:, a, :], acc[a][:, :], rstd[:, a:a + 1], None, ALU.mult
                                            ).then_inc(acc_free[a], 1)
                dve.wait_ge(acc_free[0], JOB["xbc"] + i + 2)
                dve.wait_ge(acc_free[1], JOB["xbc"] + i + 2)
                dve.nop().then_inc(filled, 1)

            def conv_job(i, out_tiles, tile0):
                conv_part("xbc", i, out_tiles, tile0, TURN["xbc"] + i - 1)
                lo_of("xbc", i, m, AHEAD + 2, m + 2)
                to_stage(i)
                lo_of("xbc", i, m, m + 2, m + AHEAD)

            lo_of("xbc", 0, m, m, m + 1)
            keep_dt()
            lo_of("xbc", 0, m, m + 1, m + 2)
            dve.wait_ge(rstd_ready, 1)
            to_stage(0)
            dt_rows()
            lo_of("xbc", 0, m, m + 2, m + 4)
            softplus()
            lo_of("xbc", 0, m, m + 4, m + AHEAD)
            lo_of("xbc", 1, m, AHEAD, AHEAD + 1)
            conv_part("xbc", 1, bc, 0, TURN["xbc"], AHEAD + 1)
            keep_sums()
            lo_of("xbc", 1, m, AHEAD + 2, m + 1)
            to_stage(1)
            lo_of("xbc", 1, m, m + 1, m + AHEAD - 1)
            keep_turned_sums()
            lo_of("xbc", 1, m, m + AHEAD - 1, m + AHEAD)
            with dve.Fori(2, 5) as i:
                st.base -= 2 * 12
                st.enter(i, 12)
                conv_job(i, bc, i * BT - BT)
            st.leave(5)
            with dve.Fori(5, CH // BLK) as i:
                st.base -= 12 * 5
                st.enter(i, 12)
                conv_job(i, xc, i * BT - 5 * BT)
            st.leave(CH // BLK)

            def turned_y(g):
                turned_lo(TURN["z"] + g, yt[:, bass.ds(g, 1), 1, :, :].rearrange("q o k n -> q (o k) n"),
                          yt[:, bass.ds(g, 1), 0, :, :].rearrange("q o k n -> q (o k) n"),
                          lambda k: gains[:, bass.ds(GAIN["ssm"] + g * BT + k, 1)])

            def z_job(g, first=False, last=False):
                dve.wait_ge(dec_in, 16 * g + 16)
                for c in range(TOK):
                    for hd in range(HG):
                        ins = nc.vector.scalar_tensor_tensor(out=dec[:, c, hd, :], in0=dec[:, c, hd, :],
                                                             scalar=cs[:, c, bass.ds(g * HG + hd, 1)],
                                                             in1=mask[:, :], op0=ALU.subtract, op1=ALU.add)
                ins.then_inc(diff_done, 1)
                if not first:
                    lo_of("z", g, m, AHEAD - 1, AHEAD)
                dve.wait_ge(exp_done, g + 1)
                dve.wait_ge(xdt_done, g + 1)
                nc.vector.tensor_tensor(xw[:, :, :], xdt[:, 0, :, :],
                                        dec[:, 0, :, P - 1:P].broadcast_to([P, HG, HD]), ALU.mult
                                        ).then_inc(xw_done, 1)
                dve.wait_ge(xw_done, g + 1)
                lo_of("z", g, m, AHEAD, AHEAD + 1)
                dve.wait_ge(bg_turn, g + 1)
                dve.wait_ge(b_kept, g + 1)
                for c in range(TOK):
                    ins = nc.vector.tensor_tensor(dec[:, c, :, :], dec[:, c, :, :],
                                                  pg[:, c * P:(c + 1) * P].rearrange("q (o l) -> q o l", o=1)
                                                  .broadcast_to([P, HG, P]), ALU.mult)
                ins.then_inc(m_done, 1)
                if first:
                    conv_part("z", g, xc, (G - 1) * BT, TURN["z"] - 1, AHEAD + 1)
                else:
                    turned_y(g - 1)
                    lo_of("z", g, m, AHEAD + 1, AHEAD + 2)
                lo_of("z", g, m, AHEAD + 2, m + 2)
                dve.wait_ge(ssd_done, g + 1)
                dve.wait_ge(skip_done, g + 1)
                nc.vector.tensor_tensor(xs[:, :, :, :].rearrange("q c h d -> q c (h d)"),
                                        xs[:, :, :, :].rearrange("q c h d -> q c (h d)"), py[:, :, :], ALU.add
                                        ).then_inc(y_sum, 1)
                dve.wait_ge(ecs_done, 1)
                nc.vector.tensor_tensor(xw[:, :, :], pst[:, :].rearrange("q (h d) -> q h d", h=HG),
                                        ecs[:, bass.ds(g * HG, HG)].rearrange("q (h o) -> q h o", o=1)
                                        .broadcast_to([P, HG, HD]), ALU.mult).then_inc(y_taken, 1)
                dve.wait_ge(y_taken, g + 2)
                dve.wait_ge(y_sum, 2 * g + 1)
                nc.vector.tensor_tensor(xs[:, 1, :, :], xs[:, 1, :, :], xw[:, :, :], ALU.add).then_inc(y_sum, 1)
                if not last:
                    dve.wait_ge(conv_out, g + 6)
                    nc.vector.tensor_copy(chan[:, :, :], xc[:, bass.ds(g * BT + BT, BT), :]).then_inc(group_in, 1)
                    nc.vector.tensor_copy(bg[:, :], bc[:, bass.ds(g + 1, 1), :]).then_inc(group_in, 1)
                    nc.vector.tensor_copy(cg[:, :], bc[:, bass.ds(g + 1 + G, 1), :]).then_inc(group_in, 1)
                lo_of("z", g, m, m + 2, m + 3)
                dve.wait_ge(y_sum, 2 * g + 2)
                dve.wait_ge(acc_free[0], JOB["z"] + g + 2)
                dve.wait_ge(acc_free[1], JOB["z"] + g + 2)
                nc.vector.tensor_tensor(stage[:, :, :], stage[:, :, :],
                                        xs[:, :, :, :].rearrange("q c h d -> q c (h d)"), ALU.mult).then_inc(gated, 1)
                dve.wait_ge(g_rstd, g + 1)
                for t in range(TOK):
                    ins = nc.vector.tensor_scalar(stage[:, t, :], stage[:, t, :], grstd[:, t:t + 1], None, ALU.mult)
                ins.then_inc(filled, 1)
                lo_of("z", g, m, m + 3, m + 4)

            z_job(0, first=True)
            with dve.Fori(1, G - 1) as g:
                z_job(g)
            z_job(G - 1, last=True)
            lo_of("wout", 0, len(inner), AHEAD - 1, AHEAD)
            turned_y(G - 1)

            def add_block(phase, i):
                for t in range(TOK):
                    bank_ready(dve, t, phase, i)
                    nc.vector.tensor_tensor(stage[:, t, :], acc[t][:, :], h[:, t, bass.ds(i * BLK, BLK)], ALU.add
                                            ).then_inc(acc_free[t], 1)
                dve.wait_ge(acc_free[0], JOB[phase] + i + 2)
                dve.wait_ge(acc_free[1], JOB[phase] + i + 2)
                dve.nop().then_inc(filled, 1)

            def update(phase, sizes, dst, high, gain):
                m = len(sizes)
                with dve.Fori(0, NB) as i:
                    lo_of(phase, i, m, AHEAD, m + 2, sizes)
                    dve.wait_ge(turn, TURN[phase] + i)
                    if UPDATE[phase]:
                        dve.wait_ge(h_kept, NB * UPDATE[phase] + i)
                    dve.wait_ge(squares, NB * (UPDATE[phase] + 1) + i)
                    if not UPDATE[phase]:
                        dve.wait_ge(rstd_ready, 1)
                    add_block(phase, i)
                    lo_of(phase, i, m, m + 2, m + AHEAD)
                    turned_lo(TURN[phase] + i, dst[:, bass.ds(i * BT, BT), :], high[:, bass.ds(i * BT, BT), :],
                              lambda k: gains[:, bass.ds(GAIN[gain] + i * BT + k, 1)])
                    if not UPDATE[phase]:
                        dve.wait_ge(h_kept, i + 1)

            def swiglu(l):
                m, name = len(full), f"gu{l}"
                with dve.Fori(0, FB) as i:
                    lo_of(name, 2 * i, m, AHEAD, 2 * m + 2)
                    for t in range(TOK):
                        dve.wait_ge(acc_free[t], JOB[name] + 2 * i + 2)
                        bank_ready(dve, t, name, 2 * i + 1)
                        nc.vector.scalar_tensor_tensor(out=stage[:, t, :], in0=acc[t][:, :],
                                                       scalar=rstd[:, t:t + 1], in1=stage[:, t, :],
                                                       op0=ALU.mult, op1=ALU.mult).then_inc(acc_free[t], 1)
                    dve.wait_ge(acc_free[0], JOB[name] + 2 * i + 3)
                    dve.wait_ge(acc_free[1], JOB[name] + 2 * i + 3)
                    dve.nop().then_inc(filled, 1)
                    lo_of(name, 2 * i, m, 2 * m + 2, 2 * m + AHEAD)
                    turned_lo(TURN[name] + i, hl[:, bass.ds(i * BT, BT), :], hh[:, bass.ds(i * BT, BT), :])

            def side_operand(l):
                dve.wait_ge(p_hi, l + 1)
                nc.vector.tensor_tensor(pl[:, :, :].rearrange("q k n -> q (k n)"), pst[:, :],
                                        ph[:, :, :].rearrange("q k n -> q (k n)").bitcast(F32), ALU.subtract
                                        ).then_inc(p_lo, 1)

            def side(l):
                c = CHUNK[f"pp{l}"]
                for b in (0, 3):
                    for t in range(TOK):
                        if t == 0:
                            dve.wait_ge(acc_done, JOB[f"pp{l}"] + b // 3 + 1)
                        else:
                            dve.wait_ge(mm_done, c + b + 1)
                        nc.vector.tensor_copy(pp[:, t, b * BLK:(b + 1) * BLK], acc[t][:, :]).then_inc(acc_free[t], 1)
                    for n in range(AHEAD, AHEAD + 1) if b == 0 else range(AHEAD + 1, AHEAD + 4):
                        lo(c + n, n)

            def gate_update(l, i, dst=None, high=None, gain=None):
                m, name = len(full), f"ple{l}"
                lo_of(name, i, m, AHEAD, m + 3)
                dve.wait_ge(acc_free[0], JOB[name] + i + 2)
                dve.wait_ge(acc_free[1], JOB[name] + i + 2)
                dve.wait_ge(side_kept, 4 * l + 4)
                step(nc.vector.tensor_tensor(stage[:, :, :], stage[:, :, :], block_of(pp, i), ALU.mult))
                done()
                nc.vector.tensor_tensor(stage[:, :, :], stage[:, :, :], block_of(h, i), ALU.add).then_inc(filled, 1)
                lo_of(name, i, m, m + 3, m + AHEAD)
                if dst is not None:
                    turned_lo(TURN[name] + i, dst[:, bass.ds(i * BT, BT), :], high[:, bass.ds(i * BT, BT), :],
                              lambda k: gains[:, bass.ds(GAIN[gain] + i * BT + k, 1)])

            def tops(n, hd):
                b = hd % 2
                dve.wait_ge(s_mm, n * BT + hd + 1)
                dve.wait_ge(mask3_done, 1)
                src = (pg, pst)[b]
                if hd >= 2:
                    dve.wait_ge(pr_turn, n * BT + hd - 1)
                step(nc.vector.tensor_tensor(sc[:, b, :], src[:, 0:3 * P], mask3[:, :], ALU.add))
                done()
                for q, (lo_, up) in enumerate(((0, P), (P, 3 * P))):
                    step(nc.vector.tensor_reduce(top[:, hd, q:q + 1], sc[:, b, lo_:up], AX.X, ALU.max))
                done()
                nc.vector.tensor_scalar(ntop[:, hd, :], top[:, hd, :], -SCALE, None, ALU.mult).then_inc(s_top, 1)

            def probs(n, hd):
                dve.wait_ge(pr_turn, n * BT + hd + 1)
                if hd >= 2:
                    dve.wait_ge(o_mm, n * BT + hd - 1)
                nc.vector.tensor_copy(prt[:, hd % 2, :, :].rearrange("q k n -> q (k n)"), py[:, 0, 0:3 * P]
                                      ).then_inc(pr_kept, 1)

            def heads_out(n, hd):
                dve.wait_ge(s_exp, 2 * (n * BT + hd) + 2)
                step(nc.vector.reciprocal(rden[:, hd, :], den[:, hd, :]))
                done()
                dve.wait_ge(o_mm, n * BT + hd + 1)
                for q in range(TOK):
                    ins = nc.vector.tensor_scalar(orow[:, q, hd * P:(hd + 1) * P],
                                                  py[:, 1, (2 * (hd % 2) + q) * P:(2 * (hd % 2) + q + 1) * P],
                                                  rden[:, hd, q:q + 1], None, ALU.mult)
                    step(ins)
                done()
                dve.nop().then_inc(o_kept, 1)

            def half_turned(t, dst):
                dve.wait_ge(turn, t + 1)
                nc.vector.tensor_copy(dst[:, 2:4, :], turned[:, 2:4, :]).then_inc(turn_dve, 1)

            update("wout", inner, ul, uh, "ffn0")
            swiglu(0)
            side_operand(0)
            update("down0", hidden, ul, uh, "ple0")
            side(0)
            with dve.Fori(0, NB) as i:
                st.enter(i, 1)
                gate_update(0, i, vl, vh, "mix1")
            st.leave(NB)
            with dve.Fori(0, NB) as i:
                lo_of("v", i, m, AHEAD, m + AHEAD)

            STEPS = 24

            def qk_pair(j, attend):
                lo_of("qk", 2 * j, m, AHEAD, m)
                if attend:
                    tops(j - 1, 0)
                    tops(j - 1, 1)
                lo_of("qk", 2 * j, m, m, m + 2)
                if attend:
                    probs(j - 1, 0)
                    tops(j - 1, 2)
                    probs(j - 1, 1)
                lo_of("qk", 2 * j, m, m + 2, m + 3)
                if attend:
                    tops(j - 1, 3)
                    heads_out(j - 1, 0)
                    probs(j - 1, 2)
                lo_of("qk", 2 * j, m, m + 3, m + 4)
                if attend:
                    heads_out(j - 1, 1)
                    probs(j - 1, 3)
                lo_of("qk", 2 * j, m, m + 4, m + AHEAD)
                if attend:
                    heads_out(j - 1, 2)
                tq = TURN["qk"] + 3 * (j - 1) + 1 if attend else TURN["q0"]
                half_turned(tq, qt)
                lo_of("qk", 2 * j, m, m + AHEAD, m + AHEAD + 1)
                if attend:
                    heads_out(j - 1, 3)
                lo_of("qk", 2 * j, m, m + AHEAD + 1, 2 * m)
                if attend:
                    turned_lo(TURN["qk"] + 3 * (j - 1) + 2, ol[:, bass.ds((j - 1) * BT, BT), :],
                              oh[:, bass.ds((j - 1) * BT, BT), :])
                lo_of("qk", 2 * j, m, 2 * m, 2 * m + AHEAD)
                half_turned(TURN["qk"] + 3 * j if attend else TURN["qk"], kt)

            qk_pair(0, False)
            with dve.Fori(1, NB) as j:
                st.base -= STEPS
                st.enter(j, STEPS)
                qk_pair(j, True)
            st.leave(NB)
            n = NB - 1
            lo_of("wo", 0, m, AHEAD, AHEAD + 1)
            tops(n, 0)
            tops(n, 1)
            probs(n, 0)
            tops(n, 2)
            lo_of("wo", 0, m, AHEAD + 1, AHEAD + 2)
            probs(n, 1)
            tops(n, 3)
            heads_out(n, 0)
            probs(n, 2)
            heads_out(n, 1)
            probs(n, 3)
            heads_out(n, 2)
            heads_out(n, 3)
            lo_of("wo", 0, m, AHEAD + 2, m)
            turned_lo(TURN["o3"], ol[:, n * BT:(n + 1) * BT, :], oh[:, n * BT:(n + 1) * BT, :])

            def wo_rest(i):
                dve.wait_ge(turn, TURN["wo"] + i)
                dve.wait_ge(squares, NB * (UPDATE["wo"] + 1) + i)
                dve.wait_ge(h_kept, NB * UPDATE["wo"] + i)
                add_block("wo", i)
                lo_of("wo", i, m, m + 2, m + AHEAD)
                turned_lo(TURN["wo"] + i, ul[:, bass.ds(i * BT, BT), :], uh[:, bass.ds(i * BT, BT), :],
                          lambda k: gains[:, bass.ds(GAIN["ffn1"] + i * BT + k, 1)])

            lo_of("wo", 0, m, m, m + 2)
            wo_rest(0)
            with dve.Fori(1, NB) as i:
                lo_of("wo", i, m, AHEAD, m + 2)
                wo_rest(i)
            swiglu(1)
            side_operand(1)
            update("down1", hidden, ul, uh, "ple1")
            side(1)
            with dve.Fori(0, NB - 1) as i:
                st.enter(i, 1)
                gate_update(1, i)
            st.leave(NB - 1)
            lo_of("ple1", NB - 1, m, AHEAD, m)
            first = (NB - 1) * BLK
            for t in range(TOK):
                dve.wait_ge(acc_free[t], JOB["ple1"] + NB + 1)
                step(nc.vector.tensor_tensor(stage[:, t, :], stage[:, t, :], pp[:, t, first:D], ALU.mult))
                done()
                nc.vector.tensor_tensor(stage[:, t, :], stage[:, t, :], h[:, t, first:D], ALU.add
                                        ).then_inc(last_sum, 1)
            dve.wait_ge(fgain_in, 16)
            for t in range(TOK):
                dve.wait_ge(last_sum, t + 1)
                nc.vector.tensor_tensor(h[:, t, first:D], stage[:, t, :], fgain[:, first:D], ALU.mult
                                        ).then_inc(last_kept, 1)
            dve.wait_ge(last_kept, TOK)
            dve.wait_ge(rstd_ready, 7)
            dve.wait_ge(h_kept, NB * 6 - 1)
            for b in range(NB):
                o = h[:, 0, b * BLK:(b + 1) * BLK]
                nc.vector.tensor_scalar(o, o, rstd[:, 0:1], None, ALU.mult).then_inc(out_ready, 1)

        @block.tensor
        def _(pe):
            def products(s, tiles, k, ah, al, banks, c, start, stop, job_=None):
                pe.wait_ge(lo_done, c + 1)
                for t in range(TOK):
                    if start and job_ is not None:
                        pe.wait_ge(acc_free[t], job_ + 1)
                    for n in range(tiles):
                        a, b = ah(k + n, t), al(k + n, t)
                        nc.tensor.matmul(banks[t], a, wh[:, s, n, :], start=start and n == 0, stop=False)
                        nc.tensor.matmul(banks[t], a, wl[:, s, n, :], start=False, stop=False)
                        ins = nc.tensor.matmul(banks[t], b, wh[:, s, n, :], start=False, stop=stop and n == tiles - 1)
                    if t == 0 and stop and job_ is not None:
                        ins.then_inc(acc_done, 1)
                ins.then_inc(mm_done, 1)

            def operand(high, low):
                return (lambda k, t: high[:, k, t * P:(t + 1) * P]), (lambda k, t: low[:, k, t * P:(t + 1) * P])

            banks = [acc[0][:, :], acc[1][:, :]]

            def job(phase, i, sizes, op, between=None, before=None):
                m, k = len(sizes), 0
                for n, size in enumerate(sizes):
                    if before and n in before:
                        before[n]()
                    c = CHUNK[phase] + i * m + n
                    products(n % RING, size, k, *op, banks, c, n == 0, n == m - 1, JOB[phase] + i)
                    k += size
                    if between and n in between:
                        between[n]()

            def turn_stage(t, src=None, wait=None):
                src = src or (lambda a, k: stage[:, a, k * P:(k + 1) * P])
                if wait:
                    wait()
                if not (isinstance(t, int) and t == 0):
                    pe.wait_ge(turn_act, t)
                    pe.wait_ge(turn_dve, t)
                for k in range(BT):
                    for a in range(TOK):
                        ins = nc.tensor.transpose(turned[:, k, a * P:(a + 1) * P], src(a, k), ident[:, :])
                ins.then_inc(turn, 1)

            def turn_fill(t, fill):
                return lambda: turn_stage(t, wait=lambda: pe.wait_ge(filled, fill + 1))

            pe.wait_ge(consts, 1)
            pe.wait_ge(small_in, 6 * 16)
            nc.tensor.transpose(acc[0][:, 0:P], grows[:, :], ident[:, :]).then_inc(gain_turn, 1)
            for n in range(CONV + 1):
                ins = nc.tensor.transpose(acc[1][:, n * CT:(n + 1) * CT], crows[:, n, :], ident[0:CT, 0:CT])
            ins.then_inc(gain_turn, 1)

            def turn_x(b):
                def _():
                    pe.wait_ge(x_in[b], 16)
                    if b >= 2:
                        pe.wait_ge(turn_dve, b - 1)
                    for k in range(BT):
                        for a in range(TOK):
                            ins = nc.tensor.transpose(half(b)[:, k, a * P:(a + 1) * P],
                                                      h[:, a, b * BLK + k * P:b * BLK + (k + 1) * P], ident[:, :])
                    ins.then_inc(turn, 1)
                return _

            def dt_product():
                pe.wait_ge(dt_lo, 1)
                o = pg[0:SH, 0:TOK * P]
                for k in range(KD):
                    nc.tensor.matmul(o, dwh[:, k, :], uh[:, k, :], start=k == 0, stop=False)
                    nc.tensor.matmul(o, dwl[:, k, :], uh[:, k, :], start=False, stop=False)
                    ins = nc.tensor.matmul(o, dwh[:, k, :], ul[:, k, :], start=False, stop=k == KD - 1)
                ins.then_inc(dt_mm, 1)

            def u_block(b):
                return lambda: pe.wait_ge(turn_dve, b + 1)

            turn_x(0)()
            turn_x(1)()
            u = operand(uh, ul)

            def turn_dt():
                pe.wait_ge(dt_kept, 1)
                for t in range(TOK):
                    ins = nc.tensor.transpose(py[:, 0, t * SH:(t + 1) * SH], dtt[:, t * P:(t + 1) * P],
                                              ident[0:SH, 0:SH])
                ins.then_inc(dt_mm, 1)

            def running_sums():
                pe.wait_ge(dta_done, 1)
                nc.tensor.matmul(py[:, 1, 0:TOK * SH], upper[:, :], dta[:, :, :].rearrange("q t h -> q (t h)"),
                                 start=True, stop=True).then_inc(cs_mm, 1)

            def turn_sums():
                pe.wait_ge(cs_kept, 1)
                nc.tensor.transpose(py[:, 1, TOK * SH:TOK * SH + P], cs[:, :, :].rearrange("q t h -> q (t h)"),
                                    ident[:, :]).then_inc(cs_mm, 1)

            job("xbc", 0, full, u, {0: turn_x(2), 2: turn_x(3), 6: dt_product, 7: turn_dt},
                {0: u_block(0), 2: u_block(1), 4: u_block(2), 6: u_block(3)})
            job("xbc", 1, full, u, {1: turn_fill(TURN["xbc"], FILL["xbc"]), 3: running_sums, 6: turn_sums})
            with pe.Fori(2, CH // BLK) as i:
                job("xbc", i, full, u, {1: turn_fill(TURN["xbc"] - 1 + i, FILL["xbc"] - 1 + i)})

            pe.wait_ge(cs_kept, 2)
            with pe.Fori(0, G) as g:
                def group_turns():
                    pe.wait_ge(group_in, 3 * g + 3)
                    pe.wait_ge(y_taken, g + 1)
                    for a in range(TOK):
                        for k in range(BT):
                            ins = nc.tensor.transpose(py[:, a, k * P:(k + 1) * P], chan[:, k, a * P:(a + 1) * P],
                                                      ident[:, :])
                    ins.then_inc(x_turn, 1)
                    pe.wait_ge(m_done, g + 1)
                    for a in range(TOK):
                        nc.tensor.matmul(pg[:, a * P:(a + 1) * P], bg[:, a * P:(a + 1) * P], cg[:, a * P:(a + 1) * P],
                                         start=True, stop=True)
                    nc.tensor.transpose(pg[:, TOK * P:(TOK + 1) * P], bg[:, 0:P], ident[:, :]).then_inc(bg_turn, 1)

                def chunk_state():
                    pe.wait_ge(xw_done, g + 1)
                    pe.wait_ge(b_kept, g + 1)
                    nc.tensor.matmul(pst[:, :], btok[:, :], xw[:, :, :].rearrange("q h d -> q (h d)"),
                                     start=True, stop=True).then_inc(st_mm, 1)

                def outputs():
                    pe.wait_ge(st_kept, g + 1)
                    nc.tensor.matmul(pst[:, :], cg[:, P:2 * P], state[:, :], start=True, stop=True)
                    pe.wait_ge(m_done, g + 2)
                    pe.wait_ge(x_kept, g + 1)
                    for a in range(TOK):
                        for hd in range(HG):
                            ins = nc.tensor.matmul(py[:, a, hd * HD:(hd + 1) * HD], dec[:, a, hd, :],
                                                   xdt[:, a, hd, :], start=True, stop=True)
                    ins.then_inc(ssd_done, 1)

                job("z", g, full, u, {0: group_turns, 1: turn_fill(TURN["z"] - 1 + g, FILL["z"] - 1 + g),
                                      4: chunk_state, 5: outputs})

            y = ((lambda k, t: yt[:, k // BT, 0, k % BT, t * P:(t + 1) * P]),
                 (lambda k, t: yt[:, k // BT, 1, k % BT, t * P:(t + 1) * P]))

            def lagged(phase, i, sizes, op, ready):
                job(phase, i, sizes, op, {1: turn_fill(TURN[phase] - 1 + i, FILL[phase] - 1 + i), 3: ready})

            with pe.Fori(0, NB) as i:
                lagged("wout", i, inner, y, lambda: pe.wait_ge(turn_dve, TURN["wout"] + i))

            def swiglu(l):
                name = f"gu{l}"
                with pe.Fori(0, FB) as i:
                    job(name, 2 * i, full, u, {1: turn_fill(TURN[name] - 1 + i, FILL[name] - 1 + i),
                                               5: lambda: pe.wait_ge(turn_dve, TURN[name] + i)})
                    job(name, 2 * i + 1, full, u)

            def down(l):
                name = f"down{l}"
                with pe.Fori(0, NB) as i:
                    job(name, i, hidden, operand(hh, hl), {1: turn_fill(TURN[name] - 1 + i, FILL[name] - 1 + i),
                                                           7: lambda: pe.wait_ge(turn_dve, TURN[name] + i)})

            def side_operand(l):
                pe.wait_ge(p_in, 16 * (l + 1))
                for k in range(KP):
                    for a in range(TOK):
                        ins = nc.tensor.transpose(pst[:, (k * TOK + a) * P:(k * TOK + a + 1) * P],
                                                  prow[:, a, k * P:(k + 1) * P], ident[:, :])
                ins.then_inc(p_turn, 1)

            def side(l):
                pe.wait_ge(p_lo, l + 1)
                op = operand(ph, pl)
                c, j = CHUNK[f"pp{l}"], JOB[f"pp{l}"]
                products(0, CK, 0, *op, banks, c, True, True, j)
                turn_stage(TURN["down0" if l == 0 else "down1"] + NB - 1,
                           wait=lambda: pe.wait_ge(filled, FILL[f"down{l}"] + NB))
                products(1, CK, 0, *op, [py[:, 0, :], py[:, 1, :]], c + 1, True, True)
                products(2, CK, 0, *op, [pg[:, :], pst[:, :]], c + 2, True, True)
                products(3, CK, 0, *op, banks, c + 3, True, True, j + 1)

            def gate_job(l, i, between=None):
                job(f"ple{l}", i, full, u, between,
                    {6: lambda: pe.wait_ge(turn_dve, TURN[f"down{l}"] + NB)})

            swiglu(0)
            side_operand(0)
            down(0)
            side(0)
            uv = operand(vh, vl)
            gate_job(0, 0)
            with pe.Fori(1, NB) as i:
                job("ple0", i, full, u, {1: turn_fill(TURN["ple0"] - 1 + i, FILL["ple0"] - 1 + i)})
            job("v", 0, full, uv, {1: turn_fill(TURN["ple0"] + NB - 1, FILL["ple0"] + NB - 1),
                                   5: lambda: pe.wait_ge(turn_dve, TURN["ple0"] + NB)})
            with pe.Fori(1, NB) as i:
                job("v", i, full, uv)

            def scores(n, hd):
                def _():
                    if hd >= 2:
                        pe.wait_ge(s_top, n * BT + hd - 1)
                    if hd == 0:
                        pe.wait_ge(turn_act, TURN["qk"] + 3 * n + 1)
                        pe.wait_ge(turn_dve, TURN["qk"] + 3 * n + 1)
                    o = (pg, pst)[hd % 2]
                    nc.tensor.matmul(o[:, 0:P], qt[:, hd, 0:P], kt[:, hd, 0:P], start=True, stop=True)
                    nc.tensor.matmul(o[:, P:3 * P], qt[:, hd, P:2 * P], kt[:, hd, :], start=True, stop=True
                                     ).then_inc(s_mm, 1)
                return _

            def turn_probs(n, hd):
                def _():
                    pe.wait_ge(s_exp, 2 * (n * BT + hd) + 2)
                    if hd:
                        pe.wait_ge(pr_kept, n * BT + hd)
                    for k in range(3):
                        ins = nc.tensor.transpose(py[:, 0, k * P:(k + 1) * P], sc[:, hd % 2, k * P:(k + 1) * P],
                                                  ident[:, :])
                    ins.then_inc(pr_turn, 1)
                return _

            def rows(n, hd):
                def _():
                    pe.wait_ge(pr_kept, n * BT + hd + 1)
                    if hd:
                        pe.wait_ge(o_kept, n * BT + hd)
                    o = py[:, 1, 2 * (hd % 2) * P:(2 * (hd % 2) + 2) * P]
                    col = bass.ds((n * BT + hd) * P, P)
                    nc.tensor.matmul(o[:, 0:P], prt[:, hd % 2, 0, :], v[:, 0, col], start=True, stop=True)
                    nc.tensor.matmul(o[:, P:2 * P], prt[:, hd % 2, 1, :], v[:, 0, col], start=True, stop=False)
                    nc.tensor.matmul(o[:, P:2 * P], prt[:, hd % 2, 2, :], v[:, 1, col], start=False, stop=True
                                     ).then_inc(o_mm, 1)
                return _

            def turn_out(n, t):
                return lambda: turn_stage(t, src=lambda a, k: orow[:, a, k * P:(k + 1) * P],
                                          wait=lambda: pe.wait_ge(o_kept, n * BT + BT))

            def then(*fs):
                def _():
                    for f in fs:
                        f()
                return _

            job("qk", 0, full, uv)
            job("qk", 1, full, uv, {1: turn_fill(TURN["q0"], FILL["qk"])})
            with pe.Fori(1, NB) as j:
                n = j - 1
                t = TURN["qk"] + 3 * (j - 1)
                job("qk", 2 * j, full, uv, {1: turn_fill(t, FILL["qk"] + 2 * j - 1),
                                            3: then(scores(n, 0), scores(n, 1)),
                                            5: then(turn_probs(n, 0), scores(n, 2)),
                                            6: then(turn_probs(n, 1), scores(n, 3), rows(n, 0)),
                                            7: turn_probs(n, 2)})
                job("qk", 2 * j + 1, full, uv, {0: then(rows(n, 1), turn_probs(n, 3)),
                                                1: then(rows(n, 2), turn_fill(t + 1, FILL["qk"] + 2 * j)),
                                                2: rows(n, 3),
                                                4: turn_out(n, t + 2)})
            n = NB - 1
            o = operand(oh, ol)
            job("wo", 0, full, o, {1: turn_fill(TURN["k3"], FILL["qk"] + 2 * NB - 1),
                                   2: then(scores(n, 0), scores(n, 1)),
                                   3: then(turn_probs(n, 0), scores(n, 2)),
                                   4: then(turn_probs(n, 1), scores(n, 3), rows(n, 0), turn_probs(n, 2)),
                                   5: then(rows(n, 1), turn_probs(n, 3), rows(n, 2), rows(n, 3),
                                           turn_out(n, TURN["o3"]))},
                {6: lambda: pe.wait_ge(turn_dve, TURN["o3"] + 1)})
            with pe.Fori(1, NB) as i:
                job("wo", i, full, o, {1: turn_fill(TURN["wo"] - 1 + i, FILL["wo"] - 1 + i)})
            swiglu(1)
            side_operand(1)
            down(1)
            side(1)
            gate_job(1, 0)
            with pe.Fori(1, NB) as i:
                job("ple1", i, full, u)


_INS = ["x", "p", "mix_norm_g", "ffn_norm_g", "ple_norm_g", "ssm_w_in", "ssm_conv_w", "ssm_conv_b", "ssm_dt_bias",
        "ssm_a_log", "ssm_d", "ssm_norm_g", "ssm_w_out", "attn_w_qkv", "attn_w_o", "ffn_w_gate", "ffn_w_up",
        "ffn_w_down", "ple_w_proj", "ple_w_gate", "final_norm_g"]


def kernel(**inputs):
    import numpy as _np
    import concourse.bacc as _bacc
    from concourse import mybir as _mybir
    from concourse.bass_utils import run_bass_kernel_spmd as _run

    nc = _bacc.Bacc("TRN2", target_bir_lowering=False, num_devices=1)
    arrays, args = {}, []
    for name in _INS:
        a = _np.ascontiguousarray(inputs[name])
        arrays[f"in_{name}"] = a
        args.append(nc.dram_tensor(f"in_{name}", a.shape, _mybir.dt.from_np(a.dtype), kind="ExternalInput").ap())
    shape = inputs["x"].shape
    args.append(nc.dram_tensor("out_0", shape, _mybir.dt.float32, kind="ExternalOutput").ap())
    args.append(nc.dram_tensor("cs_scratch", (128, 128), _mybir.dt.float32).ap())
    trunk(nc, *args)
    r = _run(nc, [arrays], core_ids=[0])
    return r.results[0]["out_0"]
```
